# Optimizing a Trainium2 kernel written in Bass

```python
import math
import jax, jax.numpy as jnp
from jax import lax
import numpy as np

D_MODEL = 2048
BATCH = 1
SEQ = 256
DEPTH = 2

CHUNK = 64
EPS = 1e-6
RET_HEADS = 8
RET_DK = 128
RET_DV = 128
RET_QK_WIDTH = RET_HEADS * RET_DK
RET_WIDTH = RET_HEADS * RET_DV
LRU_WIDTH = D_MODEL // 2
LRU_BLOCKS = 8
LRU_BW = LRU_WIDTH // LRU_BLOCKS
CONV_WIDTH = 4
LRU_C = 8.0
HYB_IN = 2 * RET_QK_WIDTH + 2 * RET_WIDTH + 2 * LRU_WIDTH
HYB_OUT = RET_WIDTH + LRU_WIDTH
ROPE_BASE = 10000.0
ATT_HEADS = 32
ATT_KV = 4
ATT_GROUP = ATT_HEADS // ATT_KV
ATT_HD = 64
ATT_QKV = (ATT_HEADS + 2 * ATT_KV) * ATT_HD
WINDOW = 128
WIN_CHUNKS = WINDOW // CHUNK
FF = 4 * D_MODEL
N_EVEN = (DEPTH + 1) // 2
N_ODD = DEPTH // 2

kernel_name = 'hybrid_retention_rglru_swa_sink_trunk'

def rmsnorm(x, w):
    xf = x.astype(jnp.float32)
    y = xf * lax.rsqrt(jnp.mean(xf * xf, axis=-1, keepdims=True) + EPS)
    return (y * w.astype(jnp.float32)).astype(x.dtype)

def rotary(x, pos):
    half = x.shape[-1] // 2
    freqs = ROPE_BASE ** (-jnp.arange(half, dtype=jnp.float32) / half)
    ang = pos[:, None] * freqs[None, :]
    cos = jnp.cos(ang)[None, :, None, :]
    sin = jnp.sin(ang)[None, :, None, :]
    x1, x2 = x[..., :half], x[..., half:]
    return jnp.concatenate([x1 * cos - x2 * sin, x1 * sin + x2 * cos], axis=-1)

def retention(q, k, v):
    B, S, H, dk = q.shape
    dv = v.shape[-1]
    N = S // CHUNK
    log_g = jnp.log1p(-jnp.power(2.0, -5.0 - jnp.arange(H, dtype=jnp.float32)))
    j = jnp.arange(CHUNK, dtype=jnp.float32)
    dmat = jnp.exp(log_g[:, None, None] * jnp.abs(j[:, None] - j[None, :]))
    qc = q.reshape(B, N, CHUNK, H, dk)
    kc = k.reshape(B, N, CHUNK, H, dk)
    vc = v.reshape(B, N, CHUNK, H, dv)
    s_intra = jnp.einsum('bnjhd,bnlhd->bnhjl', qc, kc) * dmat[None, None]
    intra = jnp.einsum('bnhjl,bnlhe->bnjhe', s_intra, vc)
    k_dec = kc * jnp.exp(log_g[None, :] * (CHUNK - 1 - j)[:, None])[:, :, None]
    kv = jnp.einsum('bnlhd,bnlhe->nbhde', k_dec, vc)
    chunk_decay = jnp.exp(log_g * CHUNK)[None, :, None, None]

    def step(state, kv_i):
        return chunk_decay * state + kv_i, state

    _, s_before = lax.scan(step, jnp.zeros_like(kv[0]), kv)
    q_dec = qc * jnp.exp(log_g[None, :] * (j + 1.0)[:, None])[:, :, None]
    inter = jnp.einsum('bnjhd,nbhde->bnjhe', q_dec, s_before)
    return (intra + inter).reshape(B, S, H, dv)

def lru_combine(e1, e2):
    a1, b1 = e1
    a2, b2 = e2
    return a1 * a2, a2 * b1 + b2

def rg_lru_block(xb, gate, conv_w, conv_b, w_a, b_a, w_x, b_x, lam):
    B, S, W = xb.shape
    xf = xb.astype(jnp.float32)
    xp = jnp.pad(xf, ((0, 0), (CONV_WIDTH - 1, 0), (0, 0)))
    xc = conv_b.astype(jnp.float32) + xp[:, 0:S] * conv_w[0]
    for tap in range(1, CONV_WIDTH):
        xc = xc + xp[:, tap:tap + S] * conv_w[tap]
    xblk = xc.reshape(B, S, LRU_BLOCKS, LRU_BW)
    r = jax.nn.sigmoid(jnp.einsum('bsnc,ncd->bsnd', xblk, w_a.astype(jnp.float32)).reshape(B, S, W) + b_a)
    i = jax.nn.sigmoid(jnp.einsum('bsnc,ncd->bsnd', xblk, w_x.astype(jnp.float32)).reshape(B, S, W) + b_x)
    log_a = -LRU_C * r * jax.nn.softplus(-lam.astype(jnp.float32))
    a = jnp.exp(log_a)
    mult = jnp.sqrt(-jnp.expm1(2.0 * log_a))
    mult = jnp.where(jnp.arange(S)[None, :, None] == 0, 1.0, mult)
    b = mult * i * xc
    _, h = lax.associative_scan(lru_combine, (a, b), axis=1)
    return h * jax.nn.gelu(gate.astype(jnp.float32), approximate=True)

def hybrid_mixer(h, w_in, ret_norm_w, conv_w, conv_b, w_a, b_a, w_x, b_x, lam, w_out, pos):
    B, S, _ = h.shape
    proj = h @ w_in
    cuts = [RET_QK_WIDTH, 2 * RET_QK_WIDTH, 2 * RET_QK_WIDTH + RET_WIDTH,
            2 * RET_QK_WIDTH + 2 * RET_WIDTH, 2 * RET_QK_WIDTH + 2 * RET_WIDTH + LRU_WIDTH]
    q, k, v, g, xb, gate = jnp.split(proj, cuts, axis=-1)
    q = rotary(q.reshape(B, S, RET_HEADS, RET_DK).astype(jnp.float32), pos) * (RET_DK ** -0.5)
    k = rotary(k.reshape(B, S, RET_HEADS, RET_DK).astype(jnp.float32), pos)
    v = v.reshape(B, S, RET_HEADS, RET_DV).astype(jnp.float32)
    o = retention(q, k, v)
    o = o * lax.rsqrt(jnp.mean(o * o, axis=-1, keepdims=True) + EPS)
    o = o.reshape(B, S, RET_WIDTH) * ret_norm_w.astype(jnp.float32)
    ret_out = o * jax.nn.silu(g.astype(jnp.float32))
    lru_out = rg_lru_block(xb, gate, conv_w, conv_b, w_a, b_a, w_x, b_x, lam)
    merged = jnp.concatenate([ret_out, lru_out], axis=-1).astype(h.dtype)
    return merged @ w_out

def shift_chunks(t, s):
    if s == 0:
        return t
    n = t.shape[1]
    pad = [(0, 0)] * t.ndim
    pad[1] = (s, 0)
    return jnp.pad(t, pad)[:, :n]

def swa_sink_attention(h, w_qkv, sinks, w_out):
    B, S, _ = h.shape
    N = S // CHUNK
    qkv = h @ w_qkv
    q, k, v = jnp.split(qkv, [ATT_HEADS * ATT_HD, (ATT_HEADS + ATT_KV) * ATT_HD], axis=-1)
    q = q.reshape(B, N, CHUNK, ATT_KV, ATT_GROUP, ATT_HD)
    k = k.reshape(B, N, CHUNK, ATT_KV, ATT_HD)
    v = v.reshape(B, N, CHUNK, ATT_KV, ATT_HD)
    backs = list(range(WIN_CHUNKS - 1, -1, -1))
    keys = jnp.concatenate([shift_chunks(k, s) for s in backs], axis=2)
    vals = jnp.concatenate([shift_chunks(v, s) for s in backs], axis=2)
    key_back = (WIN_CHUNKS - 1) - jnp.arange(WIN_CHUNKS * CHUNK) // CHUNK
    valid = jnp.arange(N)[:, None] >= key_back[None, :]
    scores = jnp.einsum('bnqkgd,bnskd->bnkgqs', q, keys).astype(jnp.float32) * (ATT_HD ** -0.5)
    scores = jnp.where(valid[None, :, None, None, None, :], scores, -1e30)
    sink = sinks.astype(jnp.float32).reshape(ATT_KV, ATT_GROUP)[None, None, :, :, None, None]
    m = jnp.maximum(jnp.max(scores, axis=-1, keepdims=True), sink)
    p = jnp.exp(scores - m)
    probs = p / (jnp.sum(p, axis=-1, keepdims=True) + jnp.exp(sink - m))
    out = jnp.einsum('bnkgqs,bnskd->bnqkgd', probs.astype(vals.dtype), vals)
    return out.reshape(B, S, ATT_HEADS * ATT_HD) @ w_out

def sqrelu_mlp(h, w_up, w_down):
    u = jax.nn.relu(h @ w_up)
    return (u * u) @ w_down

def setup_inputs(seed: int = 0) -> dict:
    key = jax.random.key(seed)
    ks = jax.random.split(key, 20)
    f32 = jnp.float32
    nrm = lambda k, shape, scale: jax.random.normal(k, shape, f32) * scale
    u = jax.random.uniform(ks[10], (N_EVEN, LRU_WIDTH), f32, 0.9, 0.999)
    a0 = u ** (1.0 / LRU_C)
    lam = jnp.log(a0) - jnp.log1p(-a0)
    return {
        'x': nrm(ks[0], (BATCH, SEQ, D_MODEL), 1.0),
        'norm_mix_w': 1.0 + nrm(ks[1], (DEPTH, D_MODEL), 0.02),
        'norm_mlp_w': 1.0 + nrm(ks[2], (DEPTH, D_MODEL), 0.02),
        'final_norm_w': 1.0 + nrm(ks[3], (D_MODEL,), 0.02),
        'hyb_w_in': nrm(ks[4], (N_EVEN, D_MODEL, HYB_IN), D_MODEL ** -0.5),
        'ret_norm_w': 1.0 + nrm(ks[5], (N_EVEN, RET_WIDTH), 0.02),
        'lru_conv_w': nrm(ks[6], (N_EVEN, CONV_WIDTH, LRU_WIDTH), CONV_WIDTH ** -0.5),
        'lru_conv_b': nrm(ks[7], (N_EVEN, LRU_WIDTH), 0.01),
        'lru_w_a': nrm(ks[8], (N_EVEN, LRU_BLOCKS, LRU_BW, LRU_BW), LRU_BW ** -0.5),
        'lru_b_a': nrm(ks[9], (N_EVEN, LRU_WIDTH), 0.01),
        'lru_w_x': nrm(ks[11], (N_EVEN, LRU_BLOCKS, LRU_BW, LRU_BW), LRU_BW ** -0.5),
        'lru_b_x': nrm(ks[12], (N_EVEN, LRU_WIDTH), 0.01),
        'lru_lambda': lam,
        'hyb_w_out': nrm(ks[13], (N_EVEN, HYB_OUT, D_MODEL), HYB_OUT ** -0.5),
        'attn_w_qkv': nrm(ks[14], (N_ODD, D_MODEL, ATT_QKV), D_MODEL ** -0.5),
        'attn_sinks': nrm(ks[15], (N_ODD, ATT_HEADS), 0.5),
        'attn_w_out': nrm(ks[16], (N_ODD, ATT_HEADS * ATT_HD, D_MODEL), (ATT_HEADS * ATT_HD) ** -0.5),
        'mlp_w_up': nrm(ks[17], (DEPTH, D_MODEL, FF), D_MODEL ** -0.5),
        'mlp_w_down': nrm(ks[18], (DEPTH, FF, D_MODEL), FF ** -0.5),
    }

def reference(x, norm_mix_w, norm_mlp_w, final_norm_w, hyb_w_in, ret_norm_w, lru_conv_w,
              lru_conv_b, lru_w_a, lru_b_a, lru_w_x, lru_b_x, lru_lambda, hyb_w_out,
              attn_w_qkv, attn_sinks, attn_w_out, mlp_w_up, mlp_w_down):
    pos = jnp.arange(x.shape[1], dtype=jnp.float32)
    for layer in range(DEPTH):
        h = rmsnorm(x, norm_mix_w[layer])
        if layer % 2 == 0:
            e = layer // 2
            y = hybrid_mixer(h, hyb_w_in[e], ret_norm_w[e], lru_conv_w[e], lru_conv_b[e],
                             lru_w_a[e], lru_b_a[e], lru_w_x[e], lru_b_x[e], lru_lambda[e],
                             hyb_w_out[e], pos)
        else:
            o = layer // 2
            y = swa_sink_attention(h, attn_w_qkv[o], attn_sinks[o], attn_w_out[o])
        x = x + y.astype(x.dtype)
        h = rmsnorm(x, norm_mlp_w[layer])
        x = x + sqrelu_mlp(h, mlp_w_up[layer], mlp_w_down[layer]).astype(x.dtype)
    return rmsnorm(x, final_norm_w)


_drawn_inputs = setup_inputs


def setup_inputs(seed=0):
    import zlib

    import numpy as np

    out = dict(_drawn_inputs(seed))
    spreads = {}
    factors = {'norm_mix_w': 2.779,
     'final_norm_w': 8.704,
     'ret_norm_w': 6.304,
     'lru_conv_b': 3.024,
     'lru_b_a': 64.0,
     'lru_b_x': 64.0,
     'attn_sinks': 64.0,
     'norm_mlp_w': 8.0}
    for name, (base, spread) in spreads.items():
        noise = np.random.default_rng([zlib.crc32(name.encode()), seed]).standard_normal(out[name].shape)
        drawn = base * np.exp(spread * noise) if base else spread * noise
        out[name] = __import__('jax').numpy.asarray(drawn.astype(out[name].dtype))
    for name, factor in factors.items():
        out[name] = (out[name] * factor).astype(out[name].dtype)
    return out
```

```python
from contextlib import ExitStack

import numpy as np

import concourse.bass as bass
from concourse import mybir
from concourse.alu_op_type import AluOpType as ALU

ACT = mybir.ActivationFunctionType
F32 = mybir.dt.float32
F32R = mybir.dt.float32r
AX_X = mybir.AxisListType.X

P = 128
D_MODEL = 2048
SEQ = 256
TT = SEQ // P
KT = D_MODEL // P
NB = 512
COLS = D_MODEL // NB
FF = 4 * D_MODEL
CHUNKS = FF // D_MODEL
CHUNK = 64
EPS = 1e-6
RET_HEADS = 8
RET_DK = 128
HG = NB // RET_DK
LRU_BLOCKS = 8
LG = LRU_BLOCKS // 2
TAPS = 4
LRU_C = 8.0
GELU_2C = 2.0 * float(np.sqrt(2.0 / np.pi))
HD = 64
GROUP = 8
KV = 4
PAIRS = GROUP // 2
SCALE = HD ** -0.5
MASKED = -1e30
DECAY_W = SEQ + P

UNITS = 4
HALVES = 8
RING = 4
AHEAD = 4

MIX_IN = [("xb", 0), ("gate", 0), ("q", 0), ("k", 0), ("v", 0), ("g", 0),
          ("xb", 1), ("gate", 1), ("q", 1), ("k", 1), ("v", 1), ("g", 1)]
MIX_COL = {"q": 0, "k": 2, "v": 4, "g": 6, "xb": 8, "gate": 10}
RESIDUAL = [("res", j) for j in range(COLS)]


def mlp_blocks(last_kind):
    blocks = []
    for c in range(CHUNKS):
        blocks += [("up", j) for j in range(COLS)]
        blocks += [(last_kind if c == CHUNKS - 1 else "down", j) for j in range(COLS)]
    return blocks


BLOCKS = (MIX_IN + RESIDUAL + mlp_blocks("res")
          + [("kv", 0)] + [("aq", g) for g in range(KV)] + RESIDUAL + mlp_blocks("fin"))
NBLK = len(BLOCKS)
MIX_OUT0 = len(MIX_IN)
MLP0 = MIX_OUT0 + COLS
QKV0 = MLP0 + 2 * CHUNKS * COLS
ATT_OUT0 = QKV0 + 1 + KV
MLP1 = ATT_OUT0 + COLS
PERIOD = 2 * COLS
NORM_OF = [0] * MIX_OUT0 + [None] * COLS + [1] * 32 + [2] * (1 + KV) + [None] * COLS + [3] * 32
BY_ACT = {"xb", "gate", "q", "k", "v", "g", "kv", "aq", "up"}
TURNED = {"xb", "gate", "q", "k", "g", "kv", "aq", "up", "res"}
SPLIT = {"g", "up", "res"}
PLAIN = TURNED - SPLIT
FROM_STAGE = {"xb", "gate", "kv", "aq"}
STATIONARY_STARTS = ({MIX_OUT0, MLP0, QKV0, ATT_OUT0, MLP1}
                     | {m + PERIOD * c + COLS for m in (MLP0, MLP1) for c in range(CHUNKS)})
LRU_IN_SLOT = {2: 0, 3: 1, 4: 2, 5: 3, 8: 4, 9: 5, 10: 6, 11: 7}


def total(kinds, each):
    out = [0]
    for kind, _ in BLOCKS:
        out.append(out[-1] + (each if kind in kinds else 0))
    return out


INIT_HALVES = 2 * COLS
N_EVAC_ACT = total(BY_ACT, TT)
N_EVAC_DVE = total({"res", "down", "fin"}, TT)
N_TURNED = total(TURNED, 2)
N_SPLIT = total(SPLIT, 2)
N_SQUARED = total({"up"}, TT)
N_SUMS = total({"res", "fin"}, TT)


class Slot:

    def __init__(self, b, i=None):
        self.b, self.i = b, i

    def plus(self, start, per):
        return start if self.i is None else self.i * per + start

    def halves(self, n):
        return self.plus(self.b * HALVES + n, PERIOD * HALVES)

    def block(self, n=0):
        return self.plus(self.b + n, PERIOD)

    def count(self, table, at, more=0):
        x = self.b + at
        per = table[x + PERIOD] - table[x] if self.i is not None else 0
        return self.plus(table[x] + more, per)


def run_slots(engine, body):
    def line(first, last):
        for b in range(first, last):
            body(Slot(b))

    line(0, MLP0 + 1)
    with engine.Fori(0, CHUNKS - 1) as i:
        for b in range(MLP0 + 1, MLP0 + 1 + PERIOD):
            body(Slot(b, i))
    line(MLP0 + 1 + PERIOD * (CHUNKS - 1), MLP1 + 1)
    with engine.Fori(0, CHUNKS - 1) as i:
        for b in range(MLP1 + 1, MLP1 + 1 + PERIOD):
            body(Slot(b, i))
    line(MLP1 + 1 + PERIOD * (CHUNKS - 1), NBLK + 1)


def row_groups(b):
    return [0, 2, 3, 1] if MIX_OUT0 <= b < MIX_OUT0 + COLS else [0, 1, 2, 3]


def rope_table():
    half = RET_DK // 2
    freqs = (np.float32(10000.0) ** (-np.arange(half, dtype=np.float32) / np.float32(half))).astype(np.float32)
    ang = np.arange(SEQ, dtype=np.float32)[:, None] * freqs[None, :]
    return np.concatenate([np.cos(ang), np.sin(ang)], axis=1).astype(np.float32)


def decay_table():
    g = 1.0 - 2.0 ** (-5.0 - np.arange(RET_HEADS))
    l, j = np.arange(SEQ)[:, None], np.arange(SEQ)[None, :]
    sees = (l // CHUNK) <= (j // CHUNK)
    d = np.where(sees[None], g[:, None, None] ** np.abs(j - l)[None], 0.0) * RET_DK ** -0.5
    return np.concatenate([d[:, :P, :], d[:, P:, P:]], axis=2).astype(np.float32)


def build(nc, t):
    ctx = ExitStack()
    with ctx:
        def sb(name, shape, dt=F32):
            return ctx.enter_context(nc.sbuf_tensor(name, shape, dt))

        def sem(name):
            return ctx.enter_context(nc.semaphore(name))

        raw = sb("raw", [P, UNITS, KT // UNITS, NB])
        w_hi = sb("w_hi", [P, RING, 2, NB], F32R)
        w_lo = sb("w_lo", [P, RING, 2, NB], F32R)
        a_hi = sb("a_hi", [P, KT, SEQ], F32R)
        a_lo = sb("a_lo", [P, KT, SEQ], F32R)
        b_hi = sb("b_hi", [P, KT, SEQ], F32R)
        b_lo = sb("b_lo", [P, KT, SEQ], F32R)
        x = sb("x", [P, TT, D_MODEL])
        stage = sb("stage", [P, TT, NB])
        turn = sb("turn", [P, TT, NB])
        junk = sb("junk", [P, NB])
        ident = sb("ident", [P, P])
        rope = sb("rope", [P, TT, RET_DK])
        vec_rows = sb("vec_rows", [P, 2, P])
        vecs = sb("vecs", [P, 136])
        sums = sb("sums", [P, 5, TT, COLS])
        ms = sb("ms", [P, 5, TT])
        rms = sb("rms", [P, 5, TT])
        rinv = sb("rinv", [P, 5, TT])
        zero = sb("zero", [P, 1])
        soft = sb("soft", [P, 8, LRU_BLOCKS])

        AREA = 12300
        area = sb("area", [P, AREA])
        place = {"at": 0}

        def take(*shape):
            n = int(np.prod(shape))
            at = place["at"]
            place["at"] = at + n
            assert place["at"] <= AREA, (place["at"], AREA)
            v = area[:, at:at + n]
            if len(shape) == 2:
                v = v.rearrange("p (a b) -> p a b", a=shape[0])
            if len(shape) == 3:
                v = v.rearrange("p (a b c) -> p a b c", a=shape[0], b=shape[1])
            return v

        decay = take(HG, DECAY_W)
        gate_w = take(2, LG, P)
        xb_t = take(LG, TAPS - 1 + SEQ)
        gate_t = take(LG, SEQ)
        q_t = take(HG, SEQ)
        k_t = take(HG, SEQ)
        v_tok = take(TT, NB)
        o_tok = take(TT, NB)
        p_ret = take(2, DECAY_W)
        xc = take(SEQ)
        ri = take(2, SEQ)
        a_lru = take(SEQ)
        th = take(SEQ)
        h_lru = take(SEQ)
        gel = take(SEQ)
        gel2 = take(SEQ)
        ret_ms = take(TT * HG)
        ret_inv = take(TT * HG)
        sig_g = q_t.rearrange("p a b -> p (a b)").rearrange("p (t n) -> p t n", t=TT)
        rot_tmp = o_tok
        place["at"] = 0
        kk_t = take(KV, SEQ)
        qq_t = take(PAIRS, SEQ)
        v_att = take(TT, KV * HD)
        v_even = take(2, KV * HD)
        probs = take(TT, GROUP, P)
        probs_t = take(TT, GROUP, P)
        sink = take(KV, GROUP)
        mx = take(TT, GROUP)
        neg_m = take(TT, GROUP)
        den = take(TT, GROUP)
        den_s = take(TT, GROUP)
        den_i = take(TT, GROUP)
        final_w = take(D_MODEL)

        acc = ctx.enter_context(nc.psum_tensor("acc", [P, 2, TT, NB], F32))
        bank = ctx.enter_context(nc.psum_tensor("bank", [P, 4, NB], F32))

        x_loaded = [sem(f"x_loaded{j}") for j in range(COLS)]
        ident_loaded = sem("ident_loaded")
        vecs_loaded = sem("vecs_loaded")
        rope_loaded = sem("rope_loaded")
        gate_w_loaded = sem("gate_w_loaded")
        decay_loaded = sem("decay_loaded")
        late_loaded = sem("late_loaded")
        final_loaded = sem("final_loaded")
        raw_loaded = [sem(f"raw_loaded{q}") for q in range(UNITS)]
        hi_ready = sem("hi_ready")
        lo_ready = sem("lo_ready")
        half_used = sem("half_used")
        evac_act = sem("evac_act")
        evac_dve = sem("evac_dve")
        squared = sem("squared")
        rotated = sem("rotated")
        gated = sem("gated")
        turned = sem("turned")
        turned_hi = sem("turned_hi")
        turned_out = sem("turned_out")
        summed = sem("summed")
        ms_ready = sem("ms_ready")
        rms_ready = sem("rms_ready")
        rinv_ready = sem("rinv_ready")
        vecs_turned = sem("vecs_turned")
        vecs_ready = sem("vecs_ready")
        chain = sem("chain")
        pool_chain = sem("pool_chain")
        soft_abs = sem("soft_abs")
        soft_exp = sem("soft_exp")
        soft_ready = sem("soft_ready")
        zeroed = sem("zeroed")
        conv_done = sem("conv_done")
        gates_done = sem("gates_done")
        sig_done = sem("sig_done")
        a_done = sem("a_done")
        th_done = sem("th_done")
        th_safe = sem("th_safe")
        root_done = sem("root_done")
        poly_done = sem("poly_done")
        gelsig_done = sem("gelsig_done")
        gelu_done = sem("gelu_done")
        lru_done = sem("lru_done")
        lru_hi = sem("lru_hi")
        lru_lo = sem("lru_lo")
        ret_scores = sem("ret_scores")
        ret_decayed = sem("ret_decayed")
        ret_out = sem("ret_out")
        ret_evac = sem("ret_evac")
        ret_ms_ready = sem("ret_ms_ready")
        ret_rms_ready = sem("ret_rms_ready")
        sig_g_done = sem("sig_g_done")
        masked = sem("masked")
        values_ready = sem("values_ready")
        scores_done = sem("scores_done")
        max_done = sem("max_done")
        exp_done = sem("exp_done")
        probs_ready = sem("probs_ready")
        probs_turned = sem("probs_turned")
        probs_t_ready = sem("probs_t_ready")
        att_done = sem("att_done")
        att_hi = sem("att_hi")
        att_lo = sem("att_lo")
        y_ready = sem("y_ready")
        stored = sem("stored")

        V_NORM = [0, KT, 2 * KT, 3 * KT]
        V_RET, V_CONV = 4 * KT, 4 * KT + 8
        V_CB, V_BA, V_BX, V_LAM = V_CONV + 32, V_CONV + 40, V_CONV + 48, V_CONV + 56

        def vec(c):
            return vecs[:, c:c + 1]

        def next_norm(b):
            return {MIX_OUT0: 1, MLP0: 2, ATT_OUT0: 3, MLP1: 4}[
                max(s for s in (MIX_OUT0, MLP0, ATT_OUT0, MLP1) if s <= b)]

        def stationary(b):
            from_b = (MIX_OUT0 <= b < MLP0 or ATT_OUT0 <= b < MLP1
                      or BLOCKS[b][0] == "down" or (b >= MLP0 and BLOCKS[b][0] in ("res", "fin")))
            return (b_hi, b_lo) if from_b else (a_hi, a_lo)

        def target(b):
            kind, j = BLOCKS[b]
            if kind == "up":
                return b_hi, b_lo, COLS * j, None
            if kind == "g":
                return b_hi, b_lo, HG * j, V_RET + HG * j
            return a_hi, a_lo, COLS * j, V_NORM[next_norm(b)] + COLS * j

        block = ctx.enter_context(nc.Block())

        @block.sync
        def _(sp):
            x_dram = t["x"].rearrange("a (t p) d -> p (a t) d", p=P)
            sp.dma_start(ident[:, :], t["ident"]).then_inc(ident_loaded, 16)
            for j in range(COLS):
                sp.dma_start(x[:, :, j * NB:(j + 1) * NB], x_dram[:, :, j * NB:(j + 1) * NB]).then_inc(x_loaded[j], 16)

            def load(slot, view):
                for q, group in enumerate(row_groups(slot.b)):
                    if slot.b > 0:
                        sp.wait_ge(lo_ready, slot.halves(2 * q + 2 - HALVES))
                    sp.dma_start(raw[:, q], view(group)).then_inc(raw_loaded[q], 16)

            def units(w):
                return w.rearrange("(g k p) (c n) -> c g p k n", p=P, k=KT // UNITS, n=NB)

            w_in = units(t["hyb_w_in"][0])
            for b, (kind, j) in enumerate(MIX_IN):
                load(Slot(b), lambda g: w_in[MIX_COL[kind] + j, g])
            w_out = units(t["hyb_w_out"][0])
            for j in range(COLS):
                load(Slot(MIX_OUT0 + j), lambda g: w_out[j, g])

            def load_mlp(layer, first):
                up = units(t["mlp_w_up"][layer])
                down = t["mlp_w_down"][layer].rearrange(
                    "(c g k p) (j n) -> c j g p k n", p=P, k=KT // UNITS, g=UNITS, n=NB)
                with sp.Fori(0, CHUNKS) as c:
                    for j in range(COLS):
                        load(Slot(first + j, c), lambda g: up[c * COLS + j, g])
                    for j in range(COLS):
                        load(Slot(first + COLS + j, c), lambda g: down[c, j, g])

            load_mlp(0, MLP0)
            w_qkv = units(t["attn_w_qkv"][0])
            for n, c in enumerate([KV] + list(range(KV))):
                load(Slot(QKV0 + n), lambda g: w_qkv[c, g])
            w_att = units(t["attn_w_out"][0])
            for j in range(COLS):
                load(Slot(ATT_OUT0 + j), lambda g: w_att[j, g])
            load_mlp(1, MLP1)

            y_dram = t["out"].rearrange("a (t p) d -> p (a t) d", p=P)
            for j in range(COLS):
                sp.wait_ge(y_ready, TT * (j + 1))
                sp.dma_start(y_dram[:, :, j * NB:(j + 1) * NB], x[:, :, j * NB:(j + 1) * NB]).then_inc(stored, 16)
            sp.wait_ge(stored, 16 * COLS)

        @block.gpsimd
        def _(pool):
            nc.gpsimd.memset(zero[:, :], 0.0).then_inc(zeroed, 1)
            nc.gpsimd.memset(vec_rows[:, :, :], 0.0).then_inc(zeroed, 1)
            nc.gpsimd.memset(xb_t[:, :, 0:TAPS - 1], 0.0).then_inc(zeroed, 1)
            pool.wait_ge(zeroed, 3)
            rows = [("norm_mix_w", 0, 0), ("norm_mlp_w", 0, KT), ("norm_mix_w", 1, 2 * KT), ("norm_mlp_w", 1, 3 * KT)]
            for name, layer, r0 in rows:
                pool.dma_start(vec_rows[r0:r0 + KT, 0, :],
                               t[name][layer].rearrange("(k p) -> k p", p=P)).then_inc(vecs_loaded, 16)
            for name, r0, n in (("ret_norm_w", 0, 8), ("lru_conv_w", 8, 32), ("lru_conv_b", 40, 8),
                                ("lru_b_a", 48, 8), ("lru_b_x", 56, 8), ("lru_lambda", 64, 8)):
                src = t[name][0]
                src = src.rearrange("w (k p) -> (w k) p", p=P) if name == "lru_conv_w" else \
                    src.rearrange("(k p) -> k p", p=P)
                pool.dma_start(vec_rows[r0:r0 + n, 1, :], src).then_inc(vecs_loaded, 16)
            pool.dma_start(rope[:, :, :], t["rope"].rearrange("(t p) d -> p t d", p=P)).then_inc(rope_loaded, 16)

            def load_gate_w(half):
                for m, name in enumerate(("lru_w_a", "lru_w_x")):
                    pool.dma_start(gate_w[:, m], t[name][0, half * LG:(half + 1) * LG].rearrange(
                        "n c d -> c n d")).then_inc(gate_w_loaded, 16)

            def load_decay(half):
                pool.dma_start(decay[:, :, :], t["decay"][half * HG:(half + 1) * HG].rearrange(
                    "h p j -> p h j")).then_inc(decay_loaded, 16)

            load_gate_w(0)
            load_decay(0)
            links = [0]

            def link(ins):
                links[0] += 1
                ins.then_inc(pool_chain, 1)
                pool.wait_ge(pool_chain, links[0])

            for n in range(LRU_BLOCKS):
                if n == LG:
                    pool.wait_ge(gates_done, LG)
                    load_gate_w(1)
                    pool.wait_ge(ret_decayed, HG)
                    load_decay(1)
                pool.wait_ge(turned_out, INIT_HALVES + N_TURNED[1 + 6 * (n // LG) + 1])
                if n > 0:
                    pool.wait_ge(lru_done, n)
                g = gate_t[:, n % LG, :]
                link(nc.gpsimd.tensor_tensor(gel[:, :], g, g, ALU.mult))
                link(nc.gpsimd.tensor_scalar(gel[:, :], gel[:, :], 0.044715, 1.0, ALU.mult, ALU.add))
                nc.gpsimd.tensor_tensor(gel2[:, :], gel[:, :], g, ALU.mult).then_inc(poly_done, 1)
                pool.wait_ge(gelsig_done, n + 1)
                nc.gpsimd.tensor_tensor(gel2[:, :], gel[:, :], g, ALU.mult).then_inc(gelu_done, 1)
            pool.wait_ge(turned_out, INIT_HALVES + N_TURNED[MIX_OUT0])
            pool.dma_start(sink.rearrange("p g h -> p (g h)"), t["attn_sinks"][0].partition_broadcast(P)
                           ).then_inc(late_loaded, 16)
            pool.dma_start(final_w[:, :], t["final_norm_w"].partition_broadcast(P)).then_inc(final_loaded, 16)

        @block.scalar
        def _(act):
            def cut_hi(slot, n):
                d, h = divmod(n, HALVES)
                if slot.b * HALVES + n >= NBLK * HALVES:
                    return
                if h % 2 == 0:
                    act.wait_ge(raw_loaded[h // 2], slot.plus(16 * (slot.b + d + 1), 16 * PERIOD))
                if slot.b * HALVES + n >= RING:
                    act.wait_ge(half_used, slot.halves(n - RING + 1))
                nc.scalar.activation(w_hi[:, h % RING], raw[:, h // 2, 2 * (h % 2):2 * (h % 2) + 2, :],
                                     ACT.Copy).then_inc(hi_ready, 1)

            def turned_parts(hi, kt, scale, m, n_turned, n_banks):
                act.wait_ge(turned, n_turned)
                src = bank[:, n_banks, :].rearrange("p (k s) -> p k s", k=2)
                if scale is None:
                    nc.scalar.activation(hi[:, kt:kt + 2, :], src, ACT.Copy).then_inc(turned_hi, 1)
                else:
                    nc.scalar.activation(hi[:, kt, :], src[:, 0, :], ACT.Copy, scale=vec(scale))
                    nc.scalar.activation(hi[:, kt + 1, :], src[:, 1, :], ACT.Copy,
                                         scale=vec(scale + 1)).then_inc(turned_hi, 1)

            def square_sums(norm, j):
                for tt in range(TT):
                    if (norm, j, tt) != (0, 0, 0):
                        act.wait_ge(summed, TT * (COLS * norm + j) + tt)
                    nc.scalar.activation(junk[:, :], x[:, tt, j * NB:(j + 1) * NB], ACT.Square,
                                         accum_out=sums[:, norm, tt, j:j + 1]).then_inc(summed, 1)

            def root(norm):
                act.wait_ge(ms_ready, norm + 1)
                nc.scalar.activation(rms[:, norm, :], ms[:, norm, :], ACT.Sqrt).then_inc(rms_ready, 1)

            def leave(slot, kind, j):
                b = slot.b - 1
                act.wait_ge(half_used, slot.halves(0))
                norm = NORM_OF[b]
                act.wait_ge(rinv_ready, norm + 1)
                for tt in range(TT):
                    src = acc[:, b % 2, tt, :]
                    s = rinv[:, norm, tt:tt + 1]
                    if kind == "g":
                        nc.scalar.activation(sig_g[:, tt, :], src, ACT.Sigmoid, scale=s).then_inc(sig_g_done, 1)
                    if kind == "v":
                        ins = nc.scalar.activation(v_tok[:, tt, :], src, ACT.Copy, scale=s)
                    elif kind == "kv":
                        nc.scalar.activation(v_att[:, tt, :], src[:, KV * HD:], ACT.Copy, scale=s)
                        ins = nc.scalar.activation(
                            stage[:, tt, :].rearrange("p (g two d) -> p g two d", g=KV, two=2),
                            src[:, 0:KV * HD].rearrange("p (g d) -> p g d", g=KV).unsqueeze(2)
                            .broadcast_to([P, KV, 2, HD]), ACT.Copy, scale=s)
                    else:
                        ins = nc.scalar.activation(stage[:, tt, :], src, ACT.Relu if kind == "up" else ACT.Copy, scale=s)
                    ins.then_inc(evac_act, 1)

            def lru(n, k):
                if k == 4:
                    act.wait_ge(gates_done, n + 1)
                    act.wait_ge(soft_ready, 1)
                    for m, col in enumerate((V_BA, V_BX)):
                        nc.scalar.activation(ri[:, m, :], bank[:, 3, m * SEQ:(m + 1) * SEQ], ACT.Sigmoid,
                                             bias=vec(col + n)).then_inc(sig_done, 1)
                    act.wait_ge(poly_done, n + 1)
                    nc.scalar.activation(gel[:, :], gel2[:, :], ACT.Sigmoid, scale=GELU_2C).then_inc(gelsig_done, 1)
                if k == 5:
                    act.wait_ge(sig_done, 2 * n + 1)
                    nc.scalar.activation(a_lru[:, :], ri[:, 0, :], ACT.Exp,
                                         scale=soft[:, 6, n:n + 1]).then_inc(a_done, 1)
                    nc.scalar.activation(th[:, :], ri[:, 0, :], ACT.Tanh,
                                         scale=soft[:, 7, n:n + 1]).then_inc(th_done, 1)
                    act.wait_ge(th_safe, n + 1)
                    nc.scalar.activation(th[:, :], th[:, :], ACT.Sqrt).then_inc(root_done, 1)
                if k == 7:
                    act.wait_ge(lru_done, n + 1)
                    nc.scalar.activation(b_hi[:, 8 + n, :], h_lru[:, :], ACT.Copy).then_inc(lru_hi, 1)

            def retention(half, k):
                if k == 4:
                    act.wait_ge(ret_out, half + 1)
                    for tt in range(TT):
                        nc.scalar.activation(o_tok[:, tt, :], bank[:, tt, :], ACT.Copy).then_inc(ret_evac, 1)
                if k == 6:
                    act.wait_ge(ret_ms_ready, half + 1)
                    nc.scalar.activation(ret_ms[:, :], ret_ms[:, :], ACT.Sqrt).then_inc(ret_rms_ready, 1)

            def attention(g, k):
                if k in (2, 3):
                    tt = k - 2
                    n = TT * g + tt
                    act.wait_ge(max_done, n + 1)
                    for h in range(GROUP):
                        s = bank[:, 2 - 2 * tt + h // PAIRS, P * (h % PAIRS):P * (h % PAIRS) + P]
                        nc.scalar.activation(probs[:, tt, h, :], s, ACT.Exp, scale=SCALE,
                                             bias=neg_m[:, tt, h:h + 1], accum_out=den[:, tt, h:h + 1])
                    nc.scalar.activation(den_s[:, tt, :], den_s[:, tt, :], ACT.Exp).then_inc(exp_done, 1)
                if k in (5, 6):
                    tt = k - 5
                    act.wait_ge(att_done, TT * g + tt + 1)
                    nc.scalar.activation(b_hi[:, PAIRS * g:PAIRS * (g + 1), tt * P:(tt + 1) * P],
                                         bank[:, 2 - 2 * tt, :].rearrange("p (q s) -> p q s", q=PAIRS),
                                         ACT.Copy).then_inc(att_hi, 1)

            def post(slot, k):
                b = slot.b - 1
                if b < 0:
                    if k == 1:
                        root(0)
                    return
                kind, j = BLOCKS[b]
                if k == 0 and kind in BY_ACT:
                    leave(slot, kind, j)
                if k == 1 and kind in ("res", "fin"):
                    act.wait_ge(evac_dve, slot.count(N_EVAC_DVE, 0))
                    square_sums(next_norm(b), j)
                if k == 2 and kind in SPLIT:
                    hi, _, kt, scale = target(b)
                    for m in range(2):
                        turned_parts(hi, kt + 2 * m, None if scale is None else scale + 2 * m, m,
                                     slot.count(N_TURNED, -1, INIT_HALVES + m + 1), m)
                if k == 3 and kind == "res" and j == COLS - 1:
                    root(next_norm(b))

            act.wait_ge(vecs_ready, 1)
            for j in range(COLS):
                for m in range(2):
                    turned_parts(a_hi, COLS * j + 2 * m, COLS * j + 2 * m, m, 2 * j + m + 1, 2 * (j % 2) + m)
                if j < 2:
                    cut_hi(Slot(0), 2 * j)
                    cut_hi(Slot(0), 2 * j + 1)
            for j in range(COLS):
                act.wait_ge(x_loaded[j], 16)
                square_sums(0, j)

            def body(slot):
                for k in range(HALVES):
                    post(slot, k)
                    b = slot.b
                    if slot.i is None and b == 0 and k == 6:
                        act.wait_ge(soft_abs, 1)
                        nc.scalar.activation(soft[:, 1, :], soft[:, 0, :], ACT.Exp, scale=-1.0).then_inc(soft_exp, 1)
                    if slot.i is None and b - 1 >= 0 and b - 1 < NBLK:
                        kind, j = BLOCKS[b - 1]
                        if b in LRU_IN_SLOT:
                            lru(LRU_IN_SLOT[b], k)
                        if kind == "v":
                            retention(j, k)
                        if kind == "aq":
                            attention(j, k)
                    cut_hi(slot, AHEAD + k)

            run_slots(act, body)
            root(4)

        @block.vector
        def _(dve):
            links = [0]

            def link(ins):
                links[0] += 1
                ins.then_inc(chain, 1)
                dve.wait_ge(chain, links[0])

            def cut_lo(slot, n):
                h = n % HALVES
                if slot.b * HALVES + n >= NBLK * HALVES:
                    return
                dve.wait_ge(hi_ready, slot.halves(n + 1))
                nc.vector.tensor_tensor(w_lo[:, h % RING], raw[:, h // 2, 2 * (h % 2):2 * (h % 2) + 2, :],
                                        w_hi[:, h % RING].bitcast(F32), ALU.subtract).then_inc(lo_ready, 1)

            def turned_parts(hi, lo, kt, scale, n_split, n_banks):
                dve.wait_ge(turned_hi, n_split)
                src = bank[:, n_banks, :].rearrange("p (k s) -> p k s", k=2)
                if scale is None:
                    nc.vector.tensor_tensor(lo[:, kt:kt + 2, :], src, hi[:, kt:kt + 2, :].bitcast(F32),
                                            ALU.subtract).then_inc(turned_out, 1)
                else:
                    for e in range(2):
                        ins = nc.vector.scalar_tensor_tensor(
                            lo[:, kt + e, :], src[:, e, :], vec(scale + e), hi[:, kt + e, :].bitcast(F32),
                            ALU.mult, ALU.subtract)
                    ins.then_inc(turned_out, 1)

            def mean_square(norm, n_sums):
                dve.wait_ge(summed, n_sums)
                link(nc.vector.tensor_reduce(ms[:, norm, :], sums[:, norm, :, :], AX_X, ALU.add))
                nc.vector.tensor_scalar(ms[:, norm, :], ms[:, norm, :], 1.0 / D_MODEL, EPS,
                                        ALU.mult, ALU.add).then_inc(ms_ready, 1)

            def inverse(norm):
                dve.wait_ge(rms_ready, norm + 1)
                nc.vector.reciprocal(rinv[:, norm, :], rms[:, norm, :]).then_inc(rinv_ready, 1)

            def rotate():
                s = stage[:, :, :].rearrange("p t (h two d) -> p t h two d", h=HG, two=2)
                o = turn[:, :, :].rearrange("p t (h two d) -> p t h two d", h=HG, two=2)
                half = RET_DK // 2
                cos = rope[:, :, 0:half].unsqueeze(2).broadcast_to([P, TT, HG, half])
                sin = rope[:, :, half:].unsqueeze(2).broadcast_to([P, TT, HG, half])
                tmp = rot_tmp.rearrange("p t (two h d) -> p two t h d", h=HG, two=2)
                x1, x2 = s[:, :, :, 0, :], s[:, :, :, 1, :]
                y1, y2 = o[:, :, :, 0, :], o[:, :, :, 1, :]
                nc.vector.tensor_tensor(y1, x1, cos, ALU.mult)
                nc.vector.tensor_tensor(tmp[:, 0], x2, sin, ALU.mult)
                nc.vector.tensor_tensor(y2, x1, sin, ALU.mult)
                link(nc.vector.tensor_tensor(tmp[:, 1], x2, cos, ALU.mult))
                nc.vector.tensor_tensor(y1, y1, tmp[:, 0], ALU.subtract)
                nc.vector.tensor_tensor(y2, y2, tmp[:, 1], ALU.add).then_inc(rotated, 1)

            def softplus():
                lam = vecs[:, V_LAM:V_LAM + LRU_BLOCKS]
                ab, z, nl, s, s2, p, neg8, pos4 = (soft[:, i, :] for i in range(8))
                link(nc.vector.tensor_scalar(nl, lam, -1.0, None, ALU.mult))
                nc.vector.tensor_tensor(ab, lam, nl, ALU.max).then_inc(soft_abs, 1)
                dve.wait_ge(soft_exp, 1)
                link(nc.vector.tensor_scalar(s, z, 2.0, None, ALU.add))
                link(nc.vector.reciprocal(s2, s))
                link(nc.vector.tensor_tensor(s, z, s2, ALU.mult))
                link(nc.vector.tensor_tensor(s2, s, s, ALU.mult))
                link(nc.vector.tensor_scalar(p, s2, 1.0 / 15.0, None, ALU.mult))
                for odd in (13, 11, 9, 7, 5, 3):
                    link(nc.vector.scalar_tensor_tensor(p, p, 1.0 / odd, s2, ALU.add, ALU.mult))
                link(nc.vector.scalar_tensor_tensor(p, p, 1.0, s, ALU.add, ALU.mult))
                link(nc.vector.tensor_scalar(nl, nl, 0.0, None, ALU.max))
                link(nc.vector.scalar_tensor_tensor(p, p, 2.0, nl, ALU.mult, ALU.add))
                nc.vector.tensor_scalar(neg8, p, -LRU_C, None, ALU.mult)
                nc.vector.tensor_scalar(pos4, p, LRU_C / 2, None, ALU.mult).then_inc(soft_ready, 1)

            def lru(n, k):
                xb = xb_t[:, n % LG, :]
                if k == 3:
                    link(nc.vector.tensor_scalar(xc[:, :], xb[:, 0:SEQ], vec(V_CONV + n), vec(V_CB + n),
                                                 ALU.mult, ALU.add))
                    for tap in range(1, TAPS):
                        ins = nc.vector.scalar_tensor_tensor(
                            xc[:, :], xb[:, tap:tap + SEQ], vec(V_CONV + LRU_BLOCKS * tap + n), xc[:, :],
                            ALU.mult, ALU.add)
                        if tap < TAPS - 1:
                            link(ins)
                    ins.then_inc(conv_done, 1)
                if k == 5:
                    dve.wait_ge(th_done, n + 1)
                    nc.vector.tensor_scalar(th[:, :], th[:, :], 2.0 ** -116, None, ALU.max).then_inc(th_safe, 1)
                if k == 6:
                    dve.wait_ge(sig_done, 2 * n + 2)
                    link(nc.vector.tensor_tensor(xc[:, :], xc[:, :], ri[:, 1, :], ALU.mult))
                    dve.wait_ge(root_done, n + 1)
                    link(nc.vector.scalar_tensor_tensor(th[:, :], a_lru[:, :], 1.0, th[:, :], ALU.add, ALU.mult))
                    link(nc.vector.memset(th[:, 0:1], 1.0))
                    link(nc.vector.tensor_tensor(xc[:, :], xc[:, :], th[:, :], ALU.mult))
                    if n > 0:
                        dve.wait_ge(lru_hi, n)
                    link(nc.vector.tensor_tensor_scan(h_lru[:, :], a_lru[:, :], xc[:, :], 0.0, ALU.mult, ALU.add))
                    dve.wait_ge(gelu_done, n + 1)
                    nc.vector.tensor_tensor(h_lru[:, :], h_lru[:, :], gel2[:, :], ALU.mult).then_inc(lru_done, 1)
                if k == 7:
                    dve.wait_ge(lru_hi, n + 1)
                    nc.vector.tensor_tensor(b_lo[:, 8 + n, :], h_lru[:, :], b_hi[:, 8 + n, :].bitcast(F32),
                                            ALU.subtract).then_inc(lru_lo, 1)

            def retention(half, k):
                if k in (2, 3):
                    dve.wait_ge(decay_loaded, 16 * (half + 1))
                    for h in (2 * k - 4, 2 * k - 3):
                        dve.wait_ge(ret_scores, HG * half + h + 1)
                        nc.vector.tensor_tensor(p_ret[:, h % 2, :], bank[:, 2 + h % 2, 0:DECAY_W], decay[:, h, :],
                                                ALU.mult).then_inc(ret_decayed, 1)
                if k == 5:
                    dve.wait_ge(ret_evac, TT * (half + 1))
                    link(nc.vector.tensor_tensor(turn[:, :, :], o_tok[:, :, :], o_tok[:, :, :], ALU.mult))
                    link(nc.vector.tensor_reduce(
                        ret_ms[:, :], turn[:, :, :].rearrange("p t (h d) -> p (t h) d", h=HG), AX_X, ALU.add))
                    nc.vector.tensor_scalar(ret_ms[:, :], ret_ms[:, :], 1.0 / RET_DK, EPS,
                                            ALU.mult, ALU.add).then_inc(ret_ms_ready, 1)
                if k == 6:
                    dve.wait_ge(ret_rms_ready, half + 1)
                    link(nc.vector.reciprocal(ret_inv[:, :], ret_ms[:, :]))
                    o = o_tok.rearrange("p t (h d) -> p (t h) d", h=HG)
                    link(nc.vector.tensor_tensor(o, o, ret_inv[:, :].unsqueeze(2).broadcast_to([P, TT * HG, RET_DK]),
                                                 ALU.mult))

            def attention(g, k):
                def scores(tt):
                    return bank[:, 2 - 2 * tt:4 - 2 * tt, :].rearrange("p e (q s) -> p (e q) s", q=PAIRS)

                if k == 0:
                    if g > 0:
                        dve.wait_ge(att_lo, TT * g)
                    nc.vector.memset(scores(0)[0:CHUNK, :, 0:CHUNK], MASKED).then_inc(masked, 1)
                if k in (2, 3):
                    tt = k - 2
                    n = TT * g + tt
                    dve.wait_ge(scores_done, n + 1)
                    dve.wait_ge(late_loaded, 16)
                    link(nc.vector.tensor_reduce(mx[:, tt, :], scores(tt), AX_X, ALU.max))
                    by_e = sink[:, g, :].rearrange("p (q e) -> p e q", e=2)
                    m = mx[:, tt, :].rearrange("p (e q) -> p e q", e=2)
                    link(nc.vector.scalar_tensor_tensor(m, m, SCALE, by_e, ALU.mult, ALU.max))
                    nc.vector.tensor_tensor(den_s[:, tt, :].rearrange("p (e q) -> p e q", e=2), by_e, m, ALU.subtract)
                    nc.vector.tensor_scalar(neg_m[:, tt, :], mx[:, tt, :], -1.0, None,
                                            ALU.mult).then_inc(max_done, 1)
                if k in (3, 4):
                    tt = k - 3
                    n = TT * g + tt
                    dve.wait_ge(exp_done, n + 1)
                    link(nc.vector.tensor_tensor(den_i[:, tt, :], den[:, tt, :], den_s[:, tt, :], ALU.add))
                    link(nc.vector.reciprocal(den_i[:, tt, :], den_i[:, tt, :]))
                    nc.vector.tensor_tensor(probs[:, tt], probs[:, tt],
                                            den_i[:, tt, :].unsqueeze(2).broadcast_to([P, GROUP, P]),
                                            ALU.mult).then_inc(probs_ready, 1)
                if k in (4, 5):
                    tt = k - 4
                    n = TT * g + tt
                    dve.wait_ge(probs_turned, n + 1)
                    nc.vector.tensor_copy(probs_t[:, tt], scores(tt)).then_inc(probs_t_ready, 1)
                if k in (5, 6):
                    tt = k - 5
                    dve.wait_ge(att_hi, TT * g + tt + 1)
                    to = slice(PAIRS * g, PAIRS * (g + 1)), slice(tt * P, (tt + 1) * P)
                    nc.vector.tensor_tensor(b_lo[:, to[0], to[1]],
                                            bank[:, 2 - 2 * tt, :].rearrange("p (q s) -> p q s", q=PAIRS),
                                            b_hi[:, to[0], to[1]].bitcast(F32), ALU.subtract).then_inc(att_lo, 1)

            def plain_target(kind, j):
                if kind == "xb":
                    return lambda m: xb_t[:, 2 * m:2 * m + 2, TAPS - 1:]
                tile = {"gate": gate_t, "q": q_t, "k": k_t, "kv": kk_t, "aq": qq_t}[kind]
                return lambda m: tile[:, 2 * m:2 * m + 2, :]

            def post(slot, k):
                b = slot.b - 1
                if b < 0 or b >= NBLK:
                    if b < 0 and k == 0:
                        inverse(0)
                    return
                kind, j = BLOCKS[b]
                late = kind != "aq"
                if k == 0 and kind in ("res", "down", "fin"):
                    dve.wait_ge(half_used, slot.halves(0))
                    for tt in range(TT):
                        xs = x[:, tt, j * NB:(j + 1) * NB]
                        nc.vector.tensor_tensor(xs, xs, acc[:, b % 2, tt, :], ALU.add).then_inc(evac_dve, 1)
                if k == 1:
                    if kind == "up":
                        for tt in range(TT):
                            dve.wait_ge(evac_act, slot.count(N_EVAC_ACT, -1, tt + 1))
                            nc.vector.tensor_tensor(stage[:, tt, :], stage[:, tt, :], stage[:, tt, :],
                                                    ALU.mult).then_inc(squared, 1)
                    if kind in "qk":
                        dve.wait_ge(rope_loaded, 16)
                        dve.wait_ge(evac_act, slot.count(N_EVAC_ACT, 0))
                        rotate()
                    if kind == "g":
                        for tt in range(TT):
                            dve.wait_ge(evac_act, slot.count(N_EVAC_ACT, -1, tt + 1))
                            link(nc.vector.tensor_tensor(turn[:, tt, :], stage[:, tt, :], sig_g[:, tt, :], ALU.mult))
                            nc.vector.tensor_tensor(turn[:, tt, :], turn[:, tt, :], o_tok[:, tt, :],
                                                    ALU.mult).then_inc(gated, 1)
                    if kind == "kv":
                        dve.wait_ge(evac_act, slot.count(N_EVAC_ACT, 0))
                        nc.vector.memset(v_even[0:CHUNK, 0, :], 0.0)
                        nc.vector.tensor_copy(v_even[CHUNK:P, 0, :], v_att[0:CHUNK, 0, :])
                        nc.vector.tensor_copy(v_even[0:CHUNK, 1, :], v_att[CHUNK:P, 0, :])
                        nc.vector.tensor_copy(v_even[CHUNK:P, 1, :], v_att[0:CHUNK, 1, :]).then_inc(values_ready, 1)
                if k == (2 if late else 1):
                    for m in range(2):
                        if kind in SPLIT:
                            hi, lo, kt, scale = target(b)
                            turned_parts(hi, lo, kt + 2 * m, None if scale is None else scale + 2 * m,
                                         slot.count(N_SPLIT, -1, INIT_HALVES + m + 1), m)
                        elif kind in PLAIN:
                            dve.wait_ge(turned, slot.count(N_TURNED, -1, INIT_HALVES + m + 1))
                            nc.vector.tensor_copy(plain_target(kind, j)(m),
                                                  bank[:, m, :].rearrange("p (k s) -> p k s", k=2)
                                                  ).then_inc(turned_out, 1)
                if k == 3 and kind == "res" and j == COLS - 1:
                    mean_square(next_norm(b), slot.count(N_SUMS, 0, TT * COLS))
                if k == 4 and kind == "res" and j == COLS - 1:
                    inverse(next_norm(b))

            dve.wait_ge(vecs_turned, 1)
            nc.vector.tensor_copy(vecs[:, :], bank[:, 3, 0:136]).then_inc(vecs_ready, 1)
            dve.wait_ge(vecs_ready, 1)
            dve.wait_ge(zeroed, 3)
            for j in range(COLS):
                for m in range(2):
                    turned_parts(a_hi, a_lo, COLS * j + 2 * m, COLS * j + 2 * m, 2 * j + m + 1, 2 * (j % 2) + m)
                if j < 2:
                    cut_lo(Slot(0), 2 * j)
                    cut_lo(Slot(0), 2 * j + 1)
            mean_square(0, TT * COLS)

            def body(slot):
                for k in range(HALVES):
                    post(slot, k)
                    b = slot.b
                    if slot.i is None and b == 0 and k == 5:
                        softplus()
                    if slot.i is None and b - 1 >= 0 and b - 1 < NBLK:
                        kind, j = BLOCKS[b - 1]
                        if kind == "v":
                            retention(j, k)
                        if b in LRU_IN_SLOT:
                            lru(LRU_IN_SLOT[b], k)
                        if kind == "aq":
                            attention(j, k)
                    cut_lo(slot, AHEAD + k)

            run_slots(dve, body)
            mean_square(4, N_SUMS[NBLK] + TT * COLS)
            inverse(4)
            dve.wait_ge(rinv_ready, 5)
            dve.wait_ge(final_loaded, 16)
            for j in range(COLS):
                for tt in range(TT):
                    xs = x[:, tt, j * NB:(j + 1) * NB]
                    nc.vector.scalar_tensor_tensor(xs, xs, rinv[:, 4, tt:tt + 1], final_w[:, j * NB:(j + 1) * NB],
                                                   ALU.mult, ALU.mult).then_inc(y_ready, 1)

        @block.tensor
        def _(pe):
            def products(slot, k):
                b = slot.b
                hi, lo = stationary(b)
                pe.wait_ge(lo_ready, slot.halves(k + 1))
                for e in range(2):
                    kt = 4 * row_groups(b)[k // 2] + 2 * (k % 2) + e
                    wh, wl = w_hi[:, k % RING, e, :], w_lo[:, k % RING, e, :]
                    first, last = k == 0 and e == 0, k == HALVES - 1 and e == 1
                    for tt in range(TT):
                        xh, xl = (s[:, kt, tt * P:(tt + 1) * P] for s in (hi, lo))
                        a = acc[:, b % 2, tt, :]
                        nc.tensor.matmul(a, xh, wh, start=first, stop=False)
                        nc.tensor.matmul(a, xh, wl, start=False, stop=False)
                        ins = nc.tensor.matmul(a, xl, wh, start=False, stop=last)
                ins.then_inc(half_used, 1)

            def turn_block(src, banks, n_out, ready=None):
                if n_out > 0 if isinstance(n_out, int) else True:
                    pe.wait_ge(turned_out, n_out)
                for m in range(2):
                    for e in range(2):
                        for tt in range(TT):
                            c = (2 * m + e) * P
                            ins = nc.tensor.transpose(
                                bank[:, banks + m, e * SEQ + tt * P:e * SEQ + (tt + 1) * P],
                                src[:, tt, c:c + P], ident[:, :])
                    ins.then_inc(turned, 1)

            def post(slot):
                b = slot.b - 1
                kind, j = BLOCKS[b]
                if kind not in TURNED:
                    return
                if kind in FROM_STAGE:
                    pe.wait_ge(evac_act, slot.count(N_EVAC_ACT, 0))
                    src = stage
                elif kind == "up":
                    pe.wait_ge(squared, slot.count(N_SQUARED, 0))
                    src = stage
                elif kind in "qk":
                    pe.wait_ge(rotated, {("q", 0): 1, ("k", 0): 2, ("q", 1): 3, ("k", 1): 4}[(kind, j)])
                    src = turn
                elif kind == "g":
                    pe.wait_ge(gated, TT * (j + 1))
                    pe.wait_ge(ret_evac, TT * (j + 1))
                    src = turn
                else:
                    pe.wait_ge(evac_dve, slot.count(N_EVAC_DVE, 0))
                    src = x[:, :, j * NB:(j + 1) * NB]
                if kind == "aq" and j > 0:
                    pe.wait_ge(att_lo, TT * j)
                if kind == "res" and b == ATT_OUT0:
                    pe.wait_ge(att_lo, TT * KV)
                turn_block(src, 0, slot.count(N_TURNED, -1, INIT_HALVES))

            def lru_gates(n):
                pe.wait_ge(conv_done, n + 1)
                pe.wait_ge(gate_w_loaded, 32 * (n // LG + 1))
                if n > 0:
                    pe.wait_ge(sig_done, 2 * n)
                if n >= LG - 1:
                    pe.wait_ge(ret_decayed, HG * (1 if n < LRU_BLOCKS - 1 else 2))
                nc.tensor.matmul(bank[:, 3, 0:SEQ], gate_w[:, 0, n % LG, :], xc[:, :], start=True, stop=True)
                nc.tensor.matmul(bank[:, 3, SEQ:2 * SEQ], gate_w[:, 1, n % LG, :], xc[:, :],
                                 start=True, stop=True).then_inc(gates_done, 1)

            def ret_score(half, h):
                if h == 0:
                    pe.wait_ge(turned_out, INIT_HALVES + N_TURNED[4 + 6 * half])
                    pe.wait_ge(sig_done, 2 * (LG * (half + 1) - 1))
                if h >= 2:
                    pe.wait_ge(ret_decayed, HG * half + h - 1)
                s = bank[:, 2 + h % 2, :]
                nc.tensor.matmul(s[:, 0:SEQ], k_t[:, h, 0:P], q_t[:, h, :], start=True, stop=True)
                nc.tensor.matmul(s[:, SEQ:DECAY_W], k_t[:, h, P:], q_t[:, h, P:], start=True,
                                 stop=True).then_inc(ret_scores, 1)

            def ret_value(half, h):
                if h == 0:
                    pe.wait_ge(evac_act, N_EVAC_ACT[5 + 6 * half])
                pe.wait_ge(ret_decayed, HG * half + h + 1)
                p = p_ret[:, h % 2, :]
                c = slice(h * P, (h + 1) * P)
                nc.tensor.matmul(bank[:, 0, c], p[:, 0:P], v_tok[:, 0, c], start=True, stop=True)
                nc.tensor.matmul(bank[:, 1, c], p[:, P:2 * P], v_tok[:, 0, c], start=True, stop=False)
                ins = nc.tensor.matmul(bank[:, 1, c], p[:, 2 * P:], v_tok[:, 1, c], start=False, stop=True)
                if h == HG - 1:
                    ins.then_inc(ret_out, 1)

            def retention(half, k):
                for what, h in {1: [(ret_score, 0), (ret_score, 1)],
                                2: [(ret_value, 0), (ret_score, 2), (ret_value, 1), (ret_score, 3)],
                                3: [(ret_value, 2), (ret_value, 3)]}.get(k, []):
                    what(half, h)

            def att_scores(g, tt):
                if tt == 0:
                    pe.wait_ge(masked, g + 1)
                    if g > 0:
                        pe.wait_ge(att_lo, TT * g)
                    pe.wait_ge(turned_out, INIT_HALVES + N_TURNED[QKV0 + 2 + g])
                for q in range(PAIRS):
                    for e in range(2):
                        for n in (2 * tt, 2 * tt + 1):
                            first = max(n - 1, 0) * CHUNK
                            width = (n + 1) * CHUNK - first
                            rows = slice(e * HD, (e + 1) * HD)
                            ins = nc.tensor.matmul(
                                bank[(n % 2) * CHUNK:(n % 2 + 1) * CHUNK, 2 - 2 * tt + e,
                                     (q + 1) * P - width:(q + 1) * P],
                                qq_t[rows, q, n * CHUNK:(n + 1) * CHUNK],
                                kk_t[rows, g, first:first + width], start=True, stop=True)
                ins.then_inc(scores_done, 1)

            def att_turn(g, tt):
                pe.wait_ge(probs_ready, TT * g + tt + 1)
                for h in range(GROUP):
                    ins = nc.tensor.transpose(
                        bank[:, 2 - 2 * tt + h // PAIRS, P * (h % PAIRS):P * (h % PAIRS) + P],
                        probs[:, tt, h, :], ident[:, :])
                ins.then_inc(probs_turned, 1)

            def att_value(g, tt):
                pe.wait_ge(values_ready, 1)
                pe.wait_ge(probs_t_ready, TT * g + tt + 1)
                o = bank[:, 2 - 2 * tt, :].rearrange("p (q s) -> p q s", q=PAIRS)
                for n in (2 * tt, 2 * tt + 1):
                    v = v_att[:, tt, :] if n % 2 else v_even[:, n // 2, :]
                    qs = slice((n % 2) * CHUNK, (n % 2 + 1) * CHUNK)
                    for e in range(2):
                        ins = nc.tensor.matmul(
                            o[e * HD:(e + 1) * HD, :, qs], v[:, g * HD:(g + 1) * HD],
                            probs_t[:, tt, PAIRS * e:PAIRS * (e + 1), qs], start=True, stop=True)
                ins.then_inc(att_done, 1)

            def attention(g, k):
                for what, tt in {1: [(att_scores, 0)], 2: [(att_scores, 1)], 3: [(att_turn, 0)],
                                 4: [(att_value, 0), (att_turn, 1)], 5: [(att_value, 1)]}.get(k, []):
                    what(g, tt)

            pe.wait_ge(ident_loaded, 16)
            pe.wait_ge(vecs_loaded, 160)
            nc.tensor.transpose(bank[:, 3, 0:4 * KT], vec_rows[0:4 * KT, 0, :], ident[0:4 * KT, 0:4 * KT])
            nc.tensor.transpose(bank[:, 3, 4 * KT:136], vec_rows[0:72, 1, :], ident[0:72, 0:72]).then_inc(vecs_turned, 1)
            for j in range(2):
                pe.wait_ge(x_loaded[j], 16)
                if j == 1:
                    pe.wait_ge(vecs_ready, 1)
                turn_block(x[:, :, j * NB:(j + 1) * NB], 2 * j, 0)

            def body(slot):
                b = slot.b
                if b == NBLK:
                    return
                if b >= 2:
                    if BLOCKS[b - 2][0] in BY_ACT:
                        pe.wait_ge(evac_act, slot.count(N_EVAC_ACT, -1))
                    else:
                        pe.wait_ge(evac_dve, slot.count(N_EVAC_DVE, -1))
                if b in STATIONARY_STARTS:
                    pe.wait_ge(turned_out, slot.count(N_TURNED, -1, INIT_HALVES))
                for k in range(HALVES):
                    if b == 0:
                        pe.wait_ge(turned_out, k + 1)
                    if b == MIX_OUT0 and k == 2:
                        pe.wait_ge(lru_lo, LRU_BLOCKS)
                    if b == ATT_OUT0 and k == 0:
                        pe.wait_ge(att_lo, TT * (KV - 1))
                    if b == ATT_OUT0 and k == HALVES - 2:
                        pe.wait_ge(att_lo, TT * KV)
                    if b in STATIONARY_STARTS and k == HALVES - 2:
                        pe.wait_ge(turned_out, slot.count(N_TURNED, 0, INIT_HALVES))
                    products(slot, k)
                    if b == 0 and k in (1, 3):
                        j = 2 + k // 2
                        pe.wait_ge(x_loaded[j], 16)
                        turn_block(x[:, :, j * NB:(j + 1) * NB], 2 * (j % 2), 2 * (j - 1))
                    if b > 0:
                        kind, j = BLOCKS[b - 1]
                        if k == (0 if kind == "aq" else 1):
                            post(slot)
                        if slot.i is None:
                            if kind == "v":
                                retention(j, k)
                            if b in LRU_IN_SLOT and k == 4:
                                lru_gates(LRU_IN_SLOT[b])
                            if kind == "aq":
                                attention(j, k)

            run_slots(pe, body)


_INS = ["x", "norm_mix_w", "norm_mlp_w", "final_norm_w", "hyb_w_in", "ret_norm_w", "lru_conv_w", "lru_conv_b",
        "lru_w_a", "lru_b_a", "lru_w_x", "lru_b_x", "lru_lambda", "hyb_w_out", "attn_w_qkv", "attn_sinks",
        "attn_w_out", "mlp_w_up", "mlp_w_down"]


def kernel(**inputs):
    import concourse.bacc as _bacc
    from concourse.bass_utils import run_bass_kernel_spmd as _run

    nc = _bacc.Bacc("TRN2", target_bir_lowering=False, num_devices=1)
    given = {name: np.ascontiguousarray(inputs[name]) for name in _INS}
    given |= {"ident": np.eye(P, dtype=np.float32), "rope": rope_table(), "decay": decay_table()}
    tensors, arrays = {}, {}
    for name, a in given.items():
        arrays[f"in_{name}"] = a
        tensors[name] = nc.dram_tensor(f"in_{name}", a.shape, mybir.dt.from_np(a.dtype), kind="ExternalInput").ap()
    tensors["out"] = nc.dram_tensor("out_y", (1, SEQ, D_MODEL), F32, kind="ExternalOutput").ap()
    build(nc, tensors)
    r = _run(nc, [arrays], core_ids=[0])
    return r.results[0]["out_y"]
```

```python
from contextlib import ExitStack

import numpy as np

import concourse.bass as bass
from concourse import mybir
from concourse.alu_op_type import AluOpType as ALU

ACT = mybir.ActivationFunctionType
F32 = mybir.dt.float32
F32R = mybir.dt.float32r
AX_X = mybir.AxisListType.X

P = 128
QUAD = 32
QUADRANTS = P // QUAD
D_MODEL = 2048
SEQ = 256
TT = SEQ // P
KT = D_MODEL // P
NB = 512
COLS = D_MODEL // NB
FF = 4 * D_MODEL
CHUNKS = FF // D_MODEL
CHUNK = 64
EPS = 1e-6
RET_HEADS = 8
RET_DK = 128
HG = NB // RET_DK
LRU_BLOCKS = 8
LG = LRU_BLOCKS // 2
TAPS = 4
LRU_C = 8.0
GELU_2C = 2.0 * float(np.sqrt(2.0 / np.pi))
HD = 64
GROUP = 8
KV = 4
PAIRS = GROUP // 2
SCALE = HD ** -0.5
MASKED = -1e30
DECAY_W = SEQ + P

UNITS = 4
HALVES = 8
RING = 4
AHEAD = 4

MIX_IN = [("xb", 0), ("gate", 0), ("q", 0), ("k", 0), ("v", 0), ("g", 0),
          ("xb", 1), ("gate", 1), ("q", 1), ("k", 1), ("v", 1), ("g", 1)]
MIX_COL = {"q": 0, "k": 2, "v": 4, "g": 6, "xb": 8, "gate": 10}
RESIDUAL = [("res", j) for j in range(COLS)]


def mlp_blocks(last_kind):
    blocks = []
    for c in range(CHUNKS):
        blocks += [("up", j) for j in range(COLS)]
        blocks += [(last_kind if c == CHUNKS - 1 else "down", j) for j in range(COLS)]
    return blocks


BLOCKS = (MIX_IN + RESIDUAL + mlp_blocks("res")
          + [("kv", 0)] + [("aq", g) for g in range(KV)] + RESIDUAL + mlp_blocks("fin"))
NBLK = len(BLOCKS)
MIX_OUT0 = len(MIX_IN)
MLP0 = MIX_OUT0 + COLS
QKV0 = MLP0 + 2 * CHUNKS * COLS
ATT_OUT0 = QKV0 + 1 + KV
MLP1 = ATT_OUT0 + COLS
PERIOD = 2 * COLS
MLP_BLOCKS = CHUNKS * PERIOD
NORM_OF = ([0] * MIX_OUT0 + [None] * COLS + [1] * MLP_BLOCKS
           + [2] * (1 + KV) + [None] * COLS + [3] * MLP_BLOCKS)
BY_ACT = {"xb", "gate", "q", "k", "v", "g", "kv", "aq", "up"}
TURNED = {"xb", "gate", "q", "k", "g", "kv", "aq", "up", "res"}
BY_QUADRANT = {"up", "res"}
SPLIT = {"g", "up", "res"}
PLAIN = TURNED - SPLIT
FROM_STAGE = {"xb", "gate", "kv", "aq"}
TURN_AT = {"aq": 0, "q": 3, "k": 3, "g": 4, "xb": 2, "gate": 2, "kv": 2}
QUADRANTS_AT = {"up": {1: 4, 2: 6, 3: 6}, "res": {1: 4, 2: 6, 3: 6}}
STATIONARY_STARTS = ({MIX_OUT0, MLP0, QKV0, ATT_OUT0, MLP1}
                     | {m + PERIOD * c + COLS for m in (MLP0, MLP1) for c in range(CHUNKS)})
LRU_IN_SLOT = {2: 0, 3: 1, 4: 2, 5: 3, 8: 4, 9: 5, 10: 6, 11: 7}


def lru_steps(b, k):
    return [(LRU_IN_SLOT[b - d], d * HALVES + k) for d in (1, 0) if b - d in LRU_IN_SLOT]


def att_late(g):
    return int(g < KV - 1)


def total(kinds, each):
    out = [0]
    for kind, _ in BLOCKS:
        out.append(out[-1] + (each if kind in kinds else 0))
    return out


INIT_HALVES = 2 * COLS
N_EVAC_ACT = total(BY_ACT, TT)
N_EVAC_DVE = total({"res", "down", "fin"}, TT)
N_TURNED = total(TURNED, 2)
N_SPLIT = total(SPLIT, 2)


def out_at(kind):
    return (max(QUADRANTS_AT[kind]) if kind in BY_QUADRANT else TURN_AT[kind]) + 1


N_SQUARED = total({"up"}, TT)
N_SUMS = total({"res", "fin"}, TT)


class Slot:

    def __init__(self, b, i=None):
        self.b, self.i = b, i

    def plus(self, start, per):
        return start if self.i is None else self.i * per + start

    def halves(self, n):
        return self.plus(self.b * HALVES + n, PERIOD * HALVES)

    def count(self, table, at, more=0):
        x = self.b + at
        per = table[x + PERIOD] - table[x] if self.i is not None else 0
        return self.plus(table[x] + more, per)


def run_slots(engine, body):
    def line(first, last):
        for b in range(first, last):
            body(Slot(b))

    line(0, MLP0 + 1)
    with engine.Fori(0, CHUNKS - 1) as i:
        for b in range(MLP0 + 1, MLP0 + 1 + PERIOD):
            body(Slot(b, i))
    line(MLP0 + 1 + PERIOD * (CHUNKS - 1), MLP1 + 1)
    with engine.Fori(0, CHUNKS - 1) as i:
        for b in range(MLP1 + 1, MLP1 + 1 + PERIOD):
            body(Slot(b, i))
    line(MLP1 + 1 + PERIOD * (CHUNKS - 1), NBLK + 1)


def row_groups(b):
    return [0, 2, 3, 1] if MIX_OUT0 <= b < MIX_OUT0 + COLS else [0, 1, 2, 3]


def rope_table():
    half = RET_DK // 2
    freqs = (np.float32(10000.0) ** (-np.arange(half, dtype=np.float32) / np.float32(half))).astype(np.float32)
    ang = np.arange(SEQ, dtype=np.float32)[:, None] * freqs[None, :]
    return np.concatenate([np.cos(ang), np.sin(ang)], axis=1).astype(np.float32)


def decay_table():
    g = 1.0 - 2.0 ** (-5.0 - np.arange(RET_HEADS))
    l, j = np.arange(SEQ)[:, None], np.arange(SEQ)[None, :]
    sees = (l // CHUNK) <= (j // CHUNK)
    d = np.where(sees[None], g[:, None, None] ** np.abs(j - l)[None], 0.0) * RET_DK ** -0.5
    return np.concatenate([d[:, :P, :], d[:, P:, P:]], axis=2).astype(np.float32)


def build(nc, t):
    ctx = ExitStack()
    with ctx:
        def sb(name, shape, dt=F32):
            return ctx.enter_context(nc.sbuf_tensor(name, shape, dt))

        def sem(name):
            return ctx.enter_context(nc.semaphore(name))

        raw = sb("raw", [P, UNITS, KT // UNITS, NB])
        w_hi = sb("w_hi", [P, RING, 2, NB], F32R)
        w_lo = sb("w_lo", [P, RING, 2, NB], F32R)
        a_hi = sb("a_hi", [P, KT, SEQ], F32R)
        a_lo = sb("a_lo", [P, KT, SEQ], F32R)
        b_hi = sb("b_hi", [P, KT, SEQ], F32R)
        b_lo = sb("b_lo", [P, KT, SEQ], F32R)
        x = sb("x", [P, TT, D_MODEL])
        stage = sb("stage", [P, TT, NB])
        turn = sb("turn", [P, TT, NB])
        junk = sb("junk", [P, NB])
        ident = sb("ident", [P, P])
        rope = sb("rope", [P, TT, RET_DK])
        vec_rows = sb("vec_rows", [P, 2, P])
        vecs = sb("vecs", [P, 136])
        sums = sb("sums", [P, 5, TT, COLS])
        ms = sb("ms", [P, 5, TT])
        rms = sb("rms", [P, 5, TT])
        rinv = sb("rinv", [P, 5, TT])
        soft = sb("soft", [P, 8, LRU_BLOCKS])

        AREA = 12300
        area = sb("area", [P, AREA])
        place = {"at": 0}

        def take(*shape):
            n = int(np.prod(shape))
            at = place["at"]
            place["at"] = at + n
            assert place["at"] <= AREA, (place["at"], AREA)
            v = area[:, at:at + n]
            if len(shape) == 2:
                v = v.rearrange("p (a b) -> p a b", a=shape[0])
            if len(shape) == 3:
                v = v.rearrange("p (a b c) -> p a b c", a=shape[0], b=shape[1])
            return v

        decay = take(HG, DECAY_W)
        gate_w = take(2, LG, P)
        xb_t = take(LG, TAPS - 1 + SEQ)
        gate_t = take(LG, SEQ)
        q_t = take(HG, SEQ)
        k_t = take(HG, SEQ)
        v_tok = take(TT, NB)
        o_tok = take(TT, NB)
        p_ret = take(2, DECAY_W)
        xc = take(SEQ)
        ri = take(2, SEQ)
        a_lru = take(SEQ)
        th = take(SEQ)
        h_lru = take(SEQ)
        gel = take(SEQ)
        gel2 = take(SEQ)
        ret_ms = take(TT * HG)
        ret_inv = take(TT * HG)
        sig_g = q_t.rearrange("p a b -> p (a b)").rearrange("p (t n) -> p t n", t=TT)
        rot_tmp = o_tok
        place["at"] = 0
        kk_t = take(KV, SEQ)
        qq_t = take(PAIRS, SEQ)
        v_att = take(TT, KV * HD)
        v_even = take(2, KV * HD)
        probs = take(TT, GROUP, P)
        probs_t = take(TT, GROUP, P)
        sink = take(KV, GROUP)
        mx = take(TT, GROUP)
        neg_m = take(TT, GROUP)
        den = take(TT, GROUP)
        den_s = take(TT, GROUP)
        den_i = take(TT, GROUP)
        final_w = take(D_MODEL)

        acc = ctx.enter_context(nc.psum_tensor("acc", [P, 2, TT, NB], F32))
        bank = ctx.enter_context(nc.psum_tensor("bank", [P, 4, NB], F32))

        x_loaded = [sem(f"x_loaded{j}") for j in range(COLS)]
        ident_loaded = sem("ident_loaded")
        norm0_loaded = sem("norm0_loaded")
        vecs_loaded = sem("vecs_loaded")
        rope_loaded = sem("rope_loaded")
        gate_w_loaded = sem("gate_w_loaded")
        decay_loaded = sem("decay_loaded")
        late_loaded = sem("late_loaded")
        final_loaded = sem("final_loaded")
        raw_loaded = [sem(f"raw_loaded{q}") for q in range(UNITS)]
        hi_ready = sem("hi_ready")
        lo_ready = sem("lo_ready")
        half_used = sem("half_used")
        evac_act = sem("evac_act")
        evac_dve = sem("evac_dve")
        squared = sem("squared")
        rotated = sem("rotated")
        gated = sem("gated")
        turned = sem("turned")
        turned_hi = sem("turned_hi")
        turned_out = sem("turned_out")
        summed = sem("summed")
        ms_ready = sem("ms_ready")
        rms_ready = sem("rms_ready")
        rinv_ready = sem("rinv_ready")
        vecs_turned = sem("vecs_turned")
        vecs_ready = sem("vecs_ready")
        chain = sem("chain")
        pool_chain = sem("pool_chain")
        soft_abs = sem("soft_abs")
        soft_exp = sem("soft_exp")
        soft_ready = sem("soft_ready")
        zeroed = sem("zeroed")
        conv_done = sem("conv_done")
        gates_done = sem("gates_done")
        sig_done = sem("sig_done")
        a_done = sem("a_done")
        th_done = sem("th_done")
        th_safe = sem("th_safe")
        root_done = sem("root_done")
        poly_done = sem("poly_done")
        gelsig_done = sem("gelsig_done")
        gelu_done = sem("gelu_done")
        lru_done = sem("lru_done")
        lru_hi = sem("lru_hi")
        lru_lo = sem("lru_lo")
        ret_scores = sem("ret_scores")
        ret_decayed = sem("ret_decayed")
        ret_out = sem("ret_out")
        ret_evac = sem("ret_evac")
        ret_ms_ready = sem("ret_ms_ready")
        ret_rms_ready = sem("ret_rms_ready")
        sig_g_done = sem("sig_g_done")
        masked = sem("masked")
        values_ready = sem("values_ready")
        scores_done = sem("scores_done")
        max_done = sem("max_done")
        exp_done = sem("exp_done")
        probs_ready = sem("probs_ready")
        probs_turned = sem("probs_turned")
        probs_t_ready = sem("probs_t_ready")
        att_done = sem("att_done")
        att_hi = sem("att_hi")
        att_lo = sem("att_lo")
        weighted = sem("weighted")
        y0_ready = sem("y0_ready")
        y1_ready = sem("y1_ready")
        stored = sem("stored")

        V_NORM = [0, KT, 2 * KT, 3 * KT]
        V_RET, V_CONV = 4 * KT, 4 * KT + 8
        V_CB, V_BA, V_BX, V_LAM = V_CONV + 32, V_CONV + 40, V_CONV + 48, V_CONV + 56

        def vec(c):
            return vecs[:, c:c + 1]

        def next_norm(b):
            return {MIX_OUT0: 1, MLP0: 2, ATT_OUT0: 3, MLP1: 4}[
                max(s for s in (MIX_OUT0, MLP0, ATT_OUT0, MLP1) if s <= b)]

        def stationary(b):
            from_b = (MIX_OUT0 <= b < MLP0 or ATT_OUT0 <= b < MLP1
                      or BLOCKS[b][0] == "down" or (b >= MLP0 and BLOCKS[b][0] in ("res", "fin")))
            return (b_hi, b_lo) if from_b else (a_hi, a_lo)

        def target(b):
            kind, j = BLOCKS[b]
            if kind == "up":
                return b_hi, b_lo, COLS * j, None
            if kind == "g":
                return b_hi, b_lo, HG * j, V_RET + HG * j
            return a_hi, a_lo, COLS * j, V_NORM[next_norm(b)] + COLS * j

        block = ctx.enter_context(nc.Block())

        @block.sync
        def _(sp):
            x_dram = t["x"].rearrange("a (t p) d -> p (a t) d", p=P)
            sp.dma_start(ident[:, :], t["ident"]).then_inc(ident_loaded, 16)

            def load_x(j):
                sp.dma_start(x[:, :, j * NB:(j + 1) * NB], x_dram[:, :, j * NB:(j + 1) * NB]).then_inc(x_loaded[j], 16)

            def load(slot, view):
                for q, group in enumerate(row_groups(slot.b)):
                    if slot.b == 0:
                        load_x(q)
                    else:
                        sp.wait_ge(lo_ready, slot.halves(2 * q + 2 - HALVES))
                    sp.dma_start(raw[:, q], view(group)).then_inc(raw_loaded[q], 16)

            def units(w):
                return w.rearrange("(g k p) (c n) -> c g p k n", p=P, k=KT // UNITS, n=NB)

            w_in = units(t["hyb_w_in"][0])
            for b, (kind, j) in enumerate(MIX_IN):
                load(Slot(b), lambda g: w_in[MIX_COL[kind] + j, g])
            w_out = units(t["hyb_w_out"][0])
            for j in range(COLS):
                load(Slot(MIX_OUT0 + j), lambda g: w_out[j, g])

            def load_mlp(layer, first):
                up = units(t["mlp_w_up"][layer])
                down = t["mlp_w_down"][layer].rearrange(
                    "(c g k p) (j n) -> c j g p k n", p=P, k=KT // UNITS, g=UNITS, n=NB)
                with sp.Fori(0, CHUNKS) as c:
                    for j in range(COLS):
                        load(Slot(first + j, c), lambda g: up[c * COLS + j, g])
                    for j in range(COLS):
                        load(Slot(first + COLS + j, c), lambda g: down[c, j, g])

            load_mlp(0, MLP0)
            w_qkv = units(t["attn_w_qkv"][0])
            for n, c in enumerate([KV] + list(range(KV))):
                load(Slot(QKV0 + n), lambda g: w_qkv[c, g])
            w_att = units(t["attn_w_out"][0])
            for j in range(COLS):
                load(Slot(ATT_OUT0 + j), lambda g: w_att[j, g])
            load_mlp(1, MLP1)

            y_dram = t["out"].rearrange("a (t p) d -> p (a t) d", p=P)
            for j in range(COLS):
                sp.wait_ge(y0_ready, j + 1)
                sp.wait_ge(y1_ready, j + 1)
                sp.dma_start(y_dram[:, :, j * NB:(j + 1) * NB], x[:, :, j * NB:(j + 1) * NB]).then_inc(stored, 16)
            sp.wait_ge(stored, 16 * COLS)

        @block.gpsimd
        def _(pool):
            nc.gpsimd.memset(xb_t[:, :, 0:TAPS - 1], 0.0).then_inc(zeroed, 1)
            rows = [("norm_mlp_w", 0, KT), ("norm_mix_w", 1, 2 * KT), ("norm_mlp_w", 1, 3 * KT)]
            for name, layer, r0 in rows:
                pool.dma_start(vec_rows[r0:r0 + KT, 0, :],
                               t[name][layer].rearrange("(k p) -> k p", p=P)).then_inc(vecs_loaded, 16)
            for name, r0, n in (("ret_norm_w", 0, 8), ("lru_conv_w", 8, 32), ("lru_conv_b", 40, 8),
                                ("lru_b_a", 48, 8), ("lru_b_x", 56, 8), ("lru_lambda", 64, 8)):
                src = t[name][0]
                src = src.rearrange("w (k p) -> (w k) p", p=P) if name == "lru_conv_w" else \
                    src.rearrange("(k p) -> k p", p=P)
                pool.dma_start(vec_rows[r0:r0 + n, 1, :], src).then_inc(vecs_loaded, 16)
            pool.dma_start(rope[:, :, :], t["rope"].rearrange("(t p) d -> p t d", p=P)).then_inc(rope_loaded, 16)

            def load_gate_w(half):
                for m, name in enumerate(("lru_w_a", "lru_w_x")):
                    pool.dma_start(gate_w[:, m], t[name][0, half * LG:(half + 1) * LG].rearrange(
                        "n c d -> c n d")).then_inc(gate_w_loaded, 16)

            def load_decay(half):
                pool.dma_start(decay[:, :, :], t["decay"][half * HG:(half + 1) * HG].rearrange(
                    "h p j -> p h j")).then_inc(decay_loaded, 16)

            pool.wait_ge(x_loaded[COLS - 1], 16)
            load_gate_w(0)
            load_decay(0)
            links = [0]

            def link(ins):
                links[0] += 1
                ins.then_inc(pool_chain, 1)
                pool.wait_ge(pool_chain, links[0])

            for n in range(LRU_BLOCKS):
                if n == LG:
                    pool.wait_ge(gates_done, LG)
                    load_gate_w(1)
                    pool.wait_ge(ret_decayed, HG)
                    load_decay(1)
                pool.wait_ge(turned_out, INIT_HALVES + N_TURNED[1 + 6 * (n // LG) + 1])
                if n > 0:
                    pool.wait_ge(lru_done, n)
                g = gate_t[:, n % LG, :]
                link(nc.gpsimd.tensor_tensor(gel[:, :], g, g, ALU.mult))
                link(nc.gpsimd.tensor_scalar(gel[:, :], gel[:, :], 0.044715, 1.0, ALU.mult, ALU.add))
                nc.gpsimd.tensor_tensor(gel2[:, :], gel[:, :], g, ALU.mult).then_inc(poly_done, 1)
                pool.wait_ge(gelsig_done, n + 1)
                nc.gpsimd.tensor_tensor(gel2[:, :], gel[:, :], g, ALU.mult).then_inc(gelu_done, 1)
            pool.wait_ge(turned_out, INIT_HALVES + N_TURNED[MIX_OUT0])
            pool.dma_start(sink.rearrange("p g h -> p (g h)"), t["attn_sinks"][0].partition_broadcast(P)
                           ).then_inc(late_loaded, 16)
            pool.dma_start(final_w[:, :], t["final_norm_w"].partition_broadcast(P)).then_inc(final_loaded, 16)

        @block.scalar
        def _(act):
            def cut_hi(slot, n):
                d, h = divmod(n, HALVES)
                if slot.b * HALVES + n >= NBLK * HALVES:
                    return
                if h % 2 == 0:
                    act.wait_ge(raw_loaded[h // 2], slot.plus(16 * (slot.b + d + 1), 16 * PERIOD))
                if slot.b * HALVES + n >= RING:
                    act.wait_ge(half_used, slot.halves(n - RING + 1))
                nc.scalar.activation(w_hi[:, h % RING], raw[:, h // 2, 2 * (h % 2):2 * (h % 2) + 2, :],
                                     ACT.Copy).then_inc(hi_ready, 1)

            def turned_parts(hi, kt, scale, n_turned, n_banks, by_quadrant=False):
                act.wait_ge(turned, n_turned)
                src = (turn if by_quadrant else bank)[:, n_banks, :].rearrange("p (k s) -> p k s", k=2)
                if scale is None:
                    nc.scalar.activation(hi[:, kt:kt + 2, :], src, ACT.Copy).then_inc(turned_hi, 1)
                else:
                    nc.scalar.activation(hi[:, kt, :], src[:, 0, :], ACT.Copy, scale=vec(scale))
                    nc.scalar.activation(hi[:, kt + 1, :], src[:, 1, :], ACT.Copy,
                                         scale=vec(scale + 1)).then_inc(turned_hi, 1)

            def square_sums(norm, j):
                for tt in range(TT):
                    if (norm, j, tt) != (0, 0, 0):
                        act.wait_ge(summed, TT * (COLS * norm + j) + tt)
                    nc.scalar.activation(junk[:, :], x[:, tt, j * NB:(j + 1) * NB], ACT.Square,
                                         accum_out=sums[:, norm, tt, j:j + 1]).then_inc(summed, 1)

            def root(norm):
                act.wait_ge(ms_ready, norm + 1)
                nc.scalar.activation(rms[:, norm, :], ms[:, norm, :], ACT.Sqrt).then_inc(rms_ready, 1)

            def leave(slot, kind, j):
                b = slot.b - 1
                act.wait_ge(half_used, slot.halves(0))
                norm = NORM_OF[b]
                act.wait_ge(rinv_ready, norm + 1)
                for tt in range(TT):
                    src = acc[:, b % 2, tt, :]
                    s = rinv[:, norm, tt:tt + 1]
                    if kind == "g":
                        nc.scalar.activation(sig_g[:, tt, :], src, ACT.Sigmoid, scale=s).then_inc(sig_g_done, 1)
                    if kind == "v":
                        ins = nc.scalar.activation(v_tok[:, tt, :], src, ACT.Copy, scale=s)
                    elif kind == "kv":
                        nc.scalar.activation(v_att[:, tt, :], src[:, KV * HD:], ACT.Copy, scale=s)
                        ins = nc.scalar.activation(
                            stage[:, tt, :].rearrange("p (g two d) -> p g two d", g=KV, two=2),
                            src[:, 0:KV * HD].rearrange("p (g d) -> p g d", g=KV).unsqueeze(2)
                            .broadcast_to([P, KV, 2, HD]), ACT.Copy, scale=s)
                    else:
                        ins = nc.scalar.activation(stage[:, tt, :], src, ACT.Relu if kind == "up" else ACT.Copy, scale=s)
                    ins.then_inc(evac_act, 1)
                if kind == "up":
                    for tt in range(TT):
                        act.wait_ge(evac_act, slot.count(N_EVAC_ACT, -1, tt + 1))
                        nc.scalar.activation(stage[:, tt, :], stage[:, tt, :], ACT.Square).then_inc(squared, 1)

            def lru(n, step):
                if step == 5:
                    act.wait_ge(gates_done, n + 1)
                    act.wait_ge(soft_ready, 1)
                    for m, col in enumerate((V_BA, V_BX)):
                        nc.scalar.activation(ri[:, m, :], bank[:, 3, m * SEQ:(m + 1) * SEQ], ACT.Sigmoid,
                                             bias=vec(col + n)).then_inc(sig_done, 1)
                    act.wait_ge(poly_done, n + 1)
                    nc.scalar.activation(gel[:, :], gel2[:, :], ACT.Sigmoid, scale=GELU_2C).then_inc(gelsig_done, 1)
                if step == 6:
                    act.wait_ge(sig_done, 2 * n + 1)
                    nc.scalar.activation(a_lru[:, :], ri[:, 0, :], ACT.Exp,
                                         scale=soft[:, 6, n:n + 1]).then_inc(a_done, 1)
                    nc.scalar.activation(th[:, :], ri[:, 0, :], ACT.Tanh,
                                         scale=soft[:, 7, n:n + 1]).then_inc(th_done, 1)
                if step == 7:
                    act.wait_ge(th_safe, n + 1)
                    nc.scalar.activation(th[:, :], th[:, :], ACT.Sqrt).then_inc(root_done, 1)
                if step == 9:
                    act.wait_ge(lru_done, n + 1)
                    nc.scalar.activation(b_hi[:, 8 + n, :], h_lru[:, :], ACT.Copy).then_inc(lru_hi, 1)

            def retention(half, k):
                if k == 4:
                    act.wait_ge(ret_out, half + 1)
                    for tt in range(TT):
                        nc.scalar.activation(o_tok[:, tt, :], bank[:, tt, :], ACT.Copy).then_inc(ret_evac, 1)
                if k == 6:
                    act.wait_ge(ret_ms_ready, half + 1)
                    nc.scalar.activation(ret_ms[:, :], ret_ms[:, :], ACT.Sqrt).then_inc(ret_rms_ready, 1)

            def attention(g, k):
                for tt in range(TT) if k == 3 else ():
                    n = TT * g + tt
                    act.wait_ge(max_done, n + 1)
                    for h in range(GROUP):
                        s = bank[:, 2 - 2 * tt + h // PAIRS, P * (h % PAIRS):P * (h % PAIRS) + P]
                        nc.scalar.activation(probs[:, tt, h, :], s, ACT.Exp, scale=SCALE,
                                             bias=neg_m[:, tt, h:h + 1], accum_out=den[:, tt, h:h + 1])
                    nc.scalar.activation(den_s[:, tt, :], den_s[:, tt, :], ACT.Exp).then_inc(exp_done, 1)
                for tt in range(TT) if k == 6 + att_late(g) else ():
                    act.wait_ge(att_done, TT * g + tt + 1)
                    nc.scalar.activation(b_hi[:, PAIRS * g:PAIRS * (g + 1), tt * P:(tt + 1) * P],
                                         bank[:, 2 - 2 * tt, :].rearrange("p (q s) -> p q s", q=PAIRS),
                                         ACT.Copy).then_inc(att_hi, 1)

            def post(slot, k):
                b = slot.b - 1
                if b < 0:
                    return
                kind, j = BLOCKS[b]
                if k == 0 and kind in BY_ACT:
                    leave(slot, kind, j)
                if k == 1 and kind in ("res", "fin"):
                    act.wait_ge(evac_dve, slot.count(N_EVAC_DVE, 0))
                    square_sums(next_norm(b), j)
                if kind in SPLIT and k == out_at(kind):
                    hi, _, kt, scale = target(b)
                    for m in range(2):
                        turned_parts(hi, kt + 2 * m, None if scale is None else scale + 2 * m,
                                     slot.count(N_TURNED, -1, INIT_HALVES + m + 1), m, kind in BY_QUADRANT)
                if k == 4 and kind == "res" and j == COLS - 1:
                    root(next_norm(b))

            act.dma_start(vec_rows[0:KT, 0, :],
                          t["norm_mix_w"][0].rearrange("(k p) -> k p", p=P)).then_inc(norm0_loaded, 16)

            act.wait_ge(vecs_ready, 1)
            def x_parts(j):
                for m in range(2):
                    turned_parts(a_hi, COLS * j + 2 * m, COLS * j + 2 * m, 2 * j + m + 1, 2 * (j % 2) + m)

            for j in range(2):
                x_parts(j)
                cut_hi(Slot(0), 2 * j)
                cut_hi(Slot(0), 2 * j + 1)

            def first_slot(k):
                if k in (0, 2):
                    x_parts(2 + k // 2)
                if 3 <= k < 3 + COLS:
                    square_sums(0, k - 3)
                if k == 7:
                    root(0)

            def body(slot):
                for k in range(HALVES):
                    post(slot, k)
                    b = slot.b
                    if slot.i is None and b == 0:
                        first_slot(k)
                    if slot.i is None and b == 1 and k == 4:
                        act.wait_ge(vecs_ready, 2)
                        act.wait_ge(soft_abs, 1)
                        nc.scalar.activation(soft[:, 1, :], soft[:, 0, :], ACT.Exp, scale=-1.0).then_inc(soft_exp, 1)
                    if slot.i is None and b - 1 >= 0 and b - 1 < NBLK:
                        kind, j = BLOCKS[b - 1]
                        for n, step in lru_steps(b, k):
                            lru(n, step)
                        if kind == "v":
                            retention(j, k)
                        if kind == "aq":
                            attention(j, k)
                    cut_hi(slot, AHEAD + k)

            run_slots(act, body)
            root(4)
            act.wait_ge(rinv_ready, 5)
            for j in range(COLS):
                act.wait_ge(weighted, TT * (j + 1))
                xs = x[:, 1, j * NB:(j + 1) * NB]
                nc.scalar.activation(xs, xs, ACT.Copy, scale=rinv[:, 4, 1:2]).then_inc(y1_ready, 1)

        @block.vector
        def _(dve):
            links = [0]

            def link(ins):
                links[0] += 1
                ins.then_inc(chain, 1)
                dve.wait_ge(chain, links[0])

            def cut_lo(slot, n):
                h = n % HALVES
                if slot.b * HALVES + n >= NBLK * HALVES:
                    return
                dve.wait_ge(hi_ready, slot.halves(n + 1))
                nc.vector.tensor_tensor(w_lo[:, h % RING], raw[:, h // 2, 2 * (h % 2):2 * (h % 2) + 2, :],
                                        w_hi[:, h % RING].bitcast(F32), ALU.subtract).then_inc(lo_ready, 1)

            def turned_parts(hi, lo, kt, scale, n_split, n_banks, by_quadrant=False):
                dve.wait_ge(turned_hi, n_split)
                src = (turn if by_quadrant else bank)[:, n_banks, :].rearrange("p (k s) -> p k s", k=2)
                if scale is None:
                    nc.vector.tensor_tensor(lo[:, kt:kt + 2, :], src, hi[:, kt:kt + 2, :].bitcast(F32),
                                            ALU.subtract).then_inc(turned_out, 1)
                else:
                    for e in range(2):
                        ins = nc.vector.scalar_tensor_tensor(
                            lo[:, kt + e, :], src[:, e, :], vec(scale + e), hi[:, kt + e, :].bitcast(F32),
                            ALU.mult, ALU.subtract)
                    ins.then_inc(turned_out, 1)

            def mean_square(norm, n_sums):
                dve.wait_ge(summed, n_sums)
                link(nc.vector.tensor_reduce(ms[:, norm, :], sums[:, norm, :, :], AX_X, ALU.add))
                nc.vector.tensor_scalar(ms[:, norm, :], ms[:, norm, :], 1.0 / D_MODEL, EPS,
                                        ALU.mult, ALU.add).then_inc(ms_ready, 1)

            def weigh(j):
                dve.wait_ge(final_loaded, 16)
                for tt in range(TT):
                    dve.wait_ge(summed, N_SUMS[NBLK - COLS + j] + TT * COLS + tt + 1)
                    xs = x[:, tt, j * NB:(j + 1) * NB]
                    nc.vector.tensor_tensor(xs, xs, final_w[:, j * NB:(j + 1) * NB], ALU.mult).then_inc(weighted, 1)

            def inverse(norm):
                dve.wait_ge(rms_ready, norm + 1)
                nc.vector.reciprocal(rinv[:, norm, :], rms[:, norm, :]).then_inc(rinv_ready, 1)

            def rotate():
                s = stage[:, :, :].rearrange("p t (h two d) -> p t h two d", h=HG, two=2)
                o = turn[:, :, :].rearrange("p t (h two d) -> p t h two d", h=HG, two=2)
                half = RET_DK // 2
                cos = rope[:, :, 0:half].unsqueeze(2).broadcast_to([P, TT, HG, half])
                sin = rope[:, :, half:].unsqueeze(2).broadcast_to([P, TT, HG, half])
                tmp = rot_tmp.rearrange("p t (two h d) -> p two t h d", h=HG, two=2)
                x1, x2 = s[:, :, :, 0, :], s[:, :, :, 1, :]
                y1, y2 = o[:, :, :, 0, :], o[:, :, :, 1, :]
                nc.vector.tensor_tensor(y1, x1, cos, ALU.mult)
                nc.vector.tensor_tensor(tmp[:, 0], x2, sin, ALU.mult)
                nc.vector.tensor_tensor(y2, x1, sin, ALU.mult)
                link(nc.vector.tensor_tensor(tmp[:, 1], x2, cos, ALU.mult))
                nc.vector.tensor_tensor(y1, y1, tmp[:, 0], ALU.subtract)
                nc.vector.tensor_tensor(y2, y2, tmp[:, 1], ALU.add).then_inc(rotated, 1)

            def softplus():
                lam = vecs[:, V_LAM:V_LAM + LRU_BLOCKS]
                ab, z, nl, s, s2, p, neg8, pos4 = (soft[:, i, :] for i in range(8))
                link(nc.vector.tensor_scalar(nl, lam, -1.0, None, ALU.mult))
                nc.vector.tensor_tensor(ab, lam, nl, ALU.max).then_inc(soft_abs, 1)
                dve.wait_ge(soft_exp, 1)
                link(nc.vector.tensor_scalar(s, z, 2.0, None, ALU.add))
                link(nc.vector.reciprocal(s2, s))
                link(nc.vector.tensor_tensor(s, z, s2, ALU.mult))
                link(nc.vector.tensor_tensor(s2, s, s, ALU.mult))
                link(nc.vector.tensor_scalar(p, s2, 1.0 / 15.0, None, ALU.mult))
                for odd in (13, 11, 9, 7, 5, 3):
                    link(nc.vector.scalar_tensor_tensor(p, p, 1.0 / odd, s2, ALU.add, ALU.mult))
                link(nc.vector.scalar_tensor_tensor(p, p, 1.0, s, ALU.add, ALU.mult))
                link(nc.vector.tensor_scalar(nl, nl, 0.0, None, ALU.max))
                link(nc.vector.scalar_tensor_tensor(p, p, 2.0, nl, ALU.mult, ALU.add))
                nc.vector.tensor_scalar(neg8, p, -LRU_C, None, ALU.mult)
                nc.vector.tensor_scalar(pos4, p, LRU_C / 2, None, ALU.mult).then_inc(soft_ready, 1)

            def lru(n, step):
                xb = xb_t[:, n % LG, :]
                if step == 2:
                    link(nc.vector.tensor_scalar(xc[:, :], xb[:, 0:SEQ], vec(V_CONV + n), vec(V_CB + n),
                                                 ALU.mult, ALU.add))
                    for tap in range(1, TAPS):
                        ins = nc.vector.scalar_tensor_tensor(
                            xc[:, :], xb[:, tap:tap + SEQ], vec(V_CONV + LRU_BLOCKS * tap + n), xc[:, :],
                            ALU.mult, ALU.add)
                        if tap < TAPS - 1:
                            link(ins)
                    ins.then_inc(conv_done, 1)
                if step == 6:
                    dve.wait_ge(th_done, n + 1)
                    nc.vector.tensor_scalar(th[:, :], th[:, :], 2.0 ** -116, None, ALU.max).then_inc(th_safe, 1)
                if step == 8:
                    dve.wait_ge(sig_done, 2 * n + 2)
                    link(nc.vector.tensor_tensor(xc[:, :], xc[:, :], ri[:, 1, :], ALU.mult))
                    dve.wait_ge(root_done, n + 1)
                    link(nc.vector.scalar_tensor_tensor(th[:, :], a_lru[:, :], 1.0, th[:, :], ALU.add, ALU.mult))
                    link(nc.vector.memset(th[:, 0:1], 1.0))
                    link(nc.vector.tensor_tensor(xc[:, :], xc[:, :], th[:, :], ALU.mult))
                    if n > 0:
                        dve.wait_ge(lru_hi, n)
                    link(nc.vector.tensor_tensor_scan(h_lru[:, :], a_lru[:, :], xc[:, :], 0.0, ALU.mult, ALU.add))
                    dve.wait_ge(gelu_done, n + 1)
                    nc.vector.tensor_tensor(h_lru[:, :], h_lru[:, :], gel2[:, :], ALU.mult).then_inc(lru_done, 1)
                if step == 9:
                    dve.wait_ge(lru_hi, n + 1)
                    nc.vector.tensor_tensor(b_lo[:, 8 + n, :], h_lru[:, :], b_hi[:, 8 + n, :].bitcast(F32),
                                            ALU.subtract).then_inc(lru_lo, 1)

            def retention(half, k):
                if k in (2, 3):
                    dve.wait_ge(decay_loaded, 16 * (half + 1))
                    for h in (2 * k - 4, 2 * k - 3):
                        dve.wait_ge(ret_scores, HG * half + h + 1)
                        nc.vector.tensor_tensor(p_ret[:, h % 2, :], bank[:, 2 + h % 2, 0:DECAY_W], decay[:, h, :],
                                                ALU.mult).then_inc(ret_decayed, 1)
                if k == 5:
                    dve.wait_ge(ret_evac, TT * (half + 1))
                    link(nc.vector.tensor_tensor(turn[:, :, :], o_tok[:, :, :], o_tok[:, :, :], ALU.mult))
                    link(nc.vector.tensor_reduce(
                        ret_ms[:, :], turn[:, :, :].rearrange("p t (h d) -> p (t h) d", h=HG), AX_X, ALU.add))
                    nc.vector.tensor_scalar(ret_ms[:, :], ret_ms[:, :], 1.0 / RET_DK, EPS,
                                            ALU.mult, ALU.add).then_inc(ret_ms_ready, 1)
                if k == 6:
                    dve.wait_ge(ret_rms_ready, half + 1)
                    link(nc.vector.reciprocal(ret_inv[:, :], ret_ms[:, :]))
                    o = o_tok.rearrange("p t (h d) -> p (t h) d", h=HG)
                    link(nc.vector.tensor_tensor(o, o, ret_inv[:, :].unsqueeze(2).broadcast_to([P, TT * HG, RET_DK]),
                                                 ALU.mult))

            def attention(g, k):
                def scores(tt):
                    return bank[:, 2 - 2 * tt:4 - 2 * tt, :].rearrange("p e (q s) -> p (e q) s", q=PAIRS)

                if k == 0:
                    if g > 0:
                        dve.wait_ge(att_lo, TT * g)
                    nc.vector.memset(scores(0)[0:CHUNK, :, 0:CHUNK], MASKED).then_inc(masked, 1)
                if k in (2, 3):
                    tt = k - 2
                    n = TT * g + tt
                    dve.wait_ge(scores_done, n + 1)
                    dve.wait_ge(late_loaded, 16)
                    link(nc.vector.tensor_reduce(mx[:, tt, :], scores(tt), AX_X, ALU.max))
                    by_e = sink[:, g, :].rearrange("p (q e) -> p e q", e=2)
                    m = mx[:, tt, :].rearrange("p (e q) -> p e q", e=2)
                    link(nc.vector.scalar_tensor_tensor(m, m, SCALE, by_e, ALU.mult, ALU.max))
                    nc.vector.tensor_tensor(den_s[:, tt, :].rearrange("p (e q) -> p e q", e=2), by_e, m, ALU.subtract)
                    nc.vector.tensor_scalar(neg_m[:, tt, :], mx[:, tt, :], -1.0, None,
                                            ALU.mult).then_inc(max_done, 1)
                for tt in range(TT) if k == 3 else ():
                    n = TT * g + tt
                    dve.wait_ge(exp_done, n + 1)
                    link(nc.vector.tensor_tensor(den_i[:, tt, :], den[:, tt, :], den_s[:, tt, :], ALU.add))
                    link(nc.vector.reciprocal(den_i[:, tt, :], den_i[:, tt, :]))
                    nc.vector.tensor_tensor(probs[:, tt], probs[:, tt],
                                            den_i[:, tt, :].unsqueeze(2).broadcast_to([P, GROUP, P]),
                                            ALU.mult).then_inc(probs_ready, 1)
                for tt in range(TT) if k == 4 + att_late(g) else ():
                    n = TT * g + tt
                    dve.wait_ge(probs_turned, n + 1)
                    nc.vector.tensor_copy(probs_t[:, tt], scores(tt)).then_inc(probs_t_ready, 1)
                for tt in range(TT) if k == 6 + att_late(g) else ():
                    dve.wait_ge(att_hi, TT * g + tt + 1)
                    to = slice(PAIRS * g, PAIRS * (g + 1)), slice(tt * P, (tt + 1) * P)
                    nc.vector.tensor_tensor(b_lo[:, to[0], to[1]],
                                            bank[:, 2 - 2 * tt, :].rearrange("p (q s) -> p q s", q=PAIRS),
                                            b_hi[:, to[0], to[1]].bitcast(F32), ALU.subtract).then_inc(att_lo, 1)

            def turn_quadrants(slot, k, kind, j):
                at = QUADRANTS_AT[kind]
                if k not in at:
                    return
                if k == min(at) and kind == "up":
                    dve.wait_ge(squared, slot.count(N_SQUARED, 0))
                if k == min(at) and kind == "res":
                    dve.wait_ge(evac_dve, slot.count(N_EVAC_DVE, 0))
                src = stage if kind == "up" else x[:, :, j * NB:(j + 1) * NB]
                src = src.rearrange("p t (k f c) -> p t k f c", k=COLS, f=QUADRANTS)
                dst = turn.rearrange("p m (k t a c) -> p t (m k) a c", k=2, t=TT, a=QUADRANTS)
                done = sum(n for tick, n in at.items() if tick < k)
                for n in range(done, done + at[k]):
                    a, f = divmod(n, QUADRANTS)
                    ins = nc.vector.transpose(dst[f * QUAD:(f + 1) * QUAD, :, :, a, :],
                                              src[a * QUAD:(a + 1) * QUAD, :, :, f, :])
                if k == max(at):
                    ins.then_inc(turned, 2)

            def plain_target(kind, j):
                if kind == "xb":
                    return lambda m: xb_t[:, 2 * m:2 * m + 2, TAPS - 1:]
                tile = {"gate": gate_t, "q": q_t, "k": k_t, "kv": kk_t, "aq": qq_t}[kind]
                return lambda m: tile[:, 2 * m:2 * m + 2, :]

            def post(slot, k):
                b = slot.b - 1
                if b < 0:
                    return
                kind, j = BLOCKS[b]
                if k == 0 and kind in ("res", "down", "fin"):
                    dve.wait_ge(half_used, slot.halves(0))
                    for tt in range(TT):
                        xs = x[:, tt, j * NB:(j + 1) * NB]
                        nc.vector.tensor_tensor(xs, xs, acc[:, b % 2, tt, :], ALU.add).then_inc(evac_dve, 1)
                if k == 1:
                    if kind in "qk":
                        dve.wait_ge(rope_loaded, 16)
                        dve.wait_ge(evac_act, slot.count(N_EVAC_ACT, 0))
                        rotate()
                    if kind == "g":
                        for tt in range(TT):
                            dve.wait_ge(evac_act, slot.count(N_EVAC_ACT, -1, tt + 1))
                            link(nc.vector.tensor_tensor(turn[:, tt, :], stage[:, tt, :], sig_g[:, tt, :], ALU.mult))
                            nc.vector.tensor_tensor(turn[:, tt, :], turn[:, tt, :], o_tok[:, tt, :],
                                                    ALU.mult).then_inc(gated, 1)
                    if kind == "kv":
                        dve.wait_ge(evac_act, slot.count(N_EVAC_ACT, 0))
                        nc.vector.memset(v_even[0:CHUNK, 0, :], 0.0)
                        nc.vector.tensor_copy(v_even[CHUNK:P, 0, :], v_att[0:CHUNK, 0, :])
                        nc.vector.tensor_copy(v_even[0:CHUNK, 1, :], v_att[CHUNK:P, 0, :])
                        nc.vector.tensor_copy(v_even[CHUNK:P, 1, :], v_att[0:CHUNK, 1, :]).then_inc(values_ready, 1)
                if kind in BY_QUADRANT:
                    turn_quadrants(slot, k, kind, j)
                if kind in TURNED and k == out_at(kind):
                    for m in range(2):
                        if kind in SPLIT:
                            hi, lo, kt, scale = target(b)
                            turned_parts(hi, lo, kt + 2 * m, None if scale is None else scale + 2 * m,
                                         slot.count(N_SPLIT, -1, INIT_HALVES + m + 1), m, kind in BY_QUADRANT)
                        elif kind in PLAIN:
                            dve.wait_ge(turned, slot.count(N_TURNED, -1, INIT_HALVES + m + 1))
                            nc.vector.tensor_copy(plain_target(kind, j)(m),
                                                  bank[:, m, :].rearrange("p (k s) -> p k s", k=2)
                                                  ).then_inc(turned_out, 1)
                if k == 3 and kind == "fin" and j < COLS - 1:
                    weigh(j)
                if k == 3 and kind == "res" and j == COLS - 1:
                    mean_square(next_norm(b), slot.count(N_SUMS, 0, TT * COLS))
                if k == 5 and kind == "res" and j == COLS - 1:
                    inverse(next_norm(b))

            dve.wait_ge(vecs_turned, 1)
            nc.vector.tensor_copy(vecs[:, 0:KT], bank[:, 3, 0:KT]).then_inc(vecs_ready, 1)
            dve.wait_ge(vecs_ready, 1)

            def x_parts(j):
                for m in range(2):
                    turned_parts(a_hi, a_lo, COLS * j + 2 * m, COLS * j + 2 * m, 2 * j + m + 1, 2 * (j % 2) + m)

            for j in range(2):
                x_parts(j)
                cut_lo(Slot(0), 2 * j)
                cut_lo(Slot(0), 2 * j + 1)

            def first_slot(k):
                if k in (0, 2):
                    x_parts(2 + k // 2)
                if k == 5:
                    dve.wait_ge(vecs_turned, 2)
                    nc.vector.tensor_copy(vecs[:, KT:136], bank[:, 2, KT:136]).then_inc(vecs_ready, 1)
                if k == 7:
                    mean_square(0, TT * COLS)

            def body(slot):
                for k in range(HALVES):
                    post(slot, k)
                    b = slot.b
                    if slot.i is None and b == 0:
                        first_slot(k)
                    if slot.i is None and b == 1 and k == 0:
                        inverse(0)
                    if slot.i is None and b == 1 and k == 4:
                        dve.wait_ge(zeroed, 1)
                        dve.wait_ge(vecs_ready, 2)
                        softplus()
                    if slot.i is None and b - 1 >= 0 and b - 1 < NBLK:
                        kind, j = BLOCKS[b - 1]
                        if kind == "v":
                            retention(j, k)
                        for n, step in lru_steps(b, k):
                            lru(n, step)
                        if kind == "aq":
                            attention(j, k)
                    cut_lo(slot, AHEAD + k)

            run_slots(dve, body)
            weigh(COLS - 1)
            mean_square(4, N_SUMS[NBLK] + TT * COLS)
            inverse(4)
            dve.wait_ge(rinv_ready, 5)
            for j in range(COLS):
                dve.wait_ge(weighted, TT * (j + 1))
                xs = x[:, 0, j * NB:(j + 1) * NB]
                nc.vector.tensor_scalar(xs, xs, rinv[:, 4, 0:1], None, ALU.mult).then_inc(y0_ready, 1)

        @block.tensor
        def _(pe):
            def products(slot, k):
                b = slot.b
                hi, lo = stationary(b)
                pe.wait_ge(lo_ready, slot.halves(k + 1))
                for e in range(2):
                    kt = 4 * row_groups(b)[k // 2] + 2 * (k % 2) + e
                    wh, wl = w_hi[:, k % RING, e, :], w_lo[:, k % RING, e, :]
                    first, last = k == 0 and e == 0, k == HALVES - 1 and e == 1
                    for tt in range(TT):
                        xh, xl = (s[:, kt, tt * P:(tt + 1) * P] for s in (hi, lo))
                        a = acc[:, b % 2, tt, :]
                        nc.tensor.matmul(a, xh, wh, start=first, stop=False)
                        nc.tensor.matmul(a, xh, wl, start=False, stop=False)
                        ins = nc.tensor.matmul(a, xl, wh, start=False, stop=last)
                ins.then_inc(half_used, 1)

            def turn_block(src, banks):
                for m in range(2):
                    for e in range(2):
                        for tt in range(TT):
                            c = (2 * m + e) * P
                            ins = nc.tensor.transpose(
                                bank[:, banks + m, e * SEQ + tt * P:e * SEQ + (tt + 1) * P],
                                src[:, tt, c:c + P], ident[:, :])
                    ins.then_inc(turned, 1)

            def post(slot):
                b = slot.b - 1
                kind, j = BLOCKS[b]
                if kind not in TURNED - BY_QUADRANT:
                    return
                if kind in FROM_STAGE:
                    pe.wait_ge(evac_act, slot.count(N_EVAC_ACT, 0))
                    src = stage
                elif kind in "qk":
                    pe.wait_ge(rotated, {("q", 0): 1, ("k", 0): 2, ("q", 1): 3, ("k", 1): 4}[(kind, j)])
                    src = turn
                else:
                    pe.wait_ge(gated, TT * (j + 1))
                    pe.wait_ge(ret_evac, TT * (j + 1))
                    src = turn
                if kind == "aq" and j > 0:
                    pe.wait_ge(att_lo, TT * j)
                pe.wait_ge(turned_out, slot.count(N_TURNED, -1, INIT_HALVES))
                turn_block(src, 0)

            def lru_gates(n):
                pe.wait_ge(conv_done, n + 1)
                pe.wait_ge(gate_w_loaded, 32 * (n // LG + 1))
                if n > 0:
                    pe.wait_ge(sig_done, 2 * n)
                if n >= LG - 1:
                    pe.wait_ge(ret_decayed, HG * (1 if n < LRU_BLOCKS - 1 else 2))
                nc.tensor.matmul(bank[:, 3, 0:SEQ], gate_w[:, 0, n % LG, :], xc[:, :], start=True, stop=True)
                nc.tensor.matmul(bank[:, 3, SEQ:2 * SEQ], gate_w[:, 1, n % LG, :], xc[:, :],
                                 start=True, stop=True).then_inc(gates_done, 1)

            def ret_score(half, h):
                if h == 0:
                    pe.wait_ge(turned_out, INIT_HALVES + N_TURNED[4 + 6 * half])
                    pe.wait_ge(sig_done, 2 * (LG * (half + 1) - 1))
                if h >= 2:
                    pe.wait_ge(ret_decayed, HG * half + h - 1)
                s = bank[:, 2 + h % 2, :]
                nc.tensor.matmul(s[:, 0:SEQ], k_t[:, h, 0:P], q_t[:, h, :], start=True, stop=True)
                nc.tensor.matmul(s[:, SEQ:DECAY_W], k_t[:, h, P:], q_t[:, h, P:], start=True,
                                 stop=True).then_inc(ret_scores, 1)

            def ret_value(half, h):
                if h == 0:
                    pe.wait_ge(evac_act, N_EVAC_ACT[5 + 6 * half])
                pe.wait_ge(ret_decayed, HG * half + h + 1)
                p = p_ret[:, h % 2, :]
                c = slice(h * P, (h + 1) * P)
                nc.tensor.matmul(bank[:, 0, c], p[:, 0:P], v_tok[:, 0, c], start=True, stop=True)
                nc.tensor.matmul(bank[:, 1, c], p[:, P:2 * P], v_tok[:, 0, c], start=True, stop=False)
                ins = nc.tensor.matmul(bank[:, 1, c], p[:, 2 * P:], v_tok[:, 1, c], start=False, stop=True)
                if h == HG - 1:
                    ins.then_inc(ret_out, 1)

            def retention(half, k):
                for what, h in {1: [(ret_score, 0), (ret_score, 1)],
                                2: [(ret_value, 0), (ret_score, 2), (ret_value, 1), (ret_score, 3)],
                                3: [(ret_value, 2), (ret_value, 3)]}.get(k, []):
                    what(half, h)

            def att_scores(g, tt):
                if tt == 0:
                    pe.wait_ge(masked, g + 1)
                    if g > 0:
                        pe.wait_ge(att_lo, TT * g)
                    pe.wait_ge(turned_out, INIT_HALVES + N_TURNED[QKV0 + 2 + g])
                for q in range(PAIRS):
                    for e in range(2):
                        for n in (2 * tt, 2 * tt + 1):
                            first = max(n - 1, 0) * CHUNK
                            width = (n + 1) * CHUNK - first
                            rows = slice(e * HD, (e + 1) * HD)
                            ins = nc.tensor.matmul(
                                bank[(n % 2) * CHUNK:(n % 2 + 1) * CHUNK, 2 - 2 * tt + e,
                                     (q + 1) * P - width:(q + 1) * P],
                                qq_t[rows, q, n * CHUNK:(n + 1) * CHUNK],
                                kk_t[rows, g, first:first + width], start=True, stop=True)
                ins.then_inc(scores_done, 1)

            def att_turn(g, tt):
                pe.wait_ge(probs_ready, TT * g + tt + 1)
                for h in range(GROUP):
                    ins = nc.tensor.transpose(
                        bank[:, 2 - 2 * tt + h // PAIRS, P * (h % PAIRS):P * (h % PAIRS) + P],
                        probs[:, tt, h, :], ident[:, :])
                ins.then_inc(probs_turned, 1)

            def att_value(g, tt):
                pe.wait_ge(values_ready, 1)
                pe.wait_ge(probs_t_ready, TT * g + tt + 1)
                o = bank[:, 2 - 2 * tt, :].rearrange("p (q s) -> p q s", q=PAIRS)
                for n in (2 * tt, 2 * tt + 1):
                    v = v_att[:, tt, :] if n % 2 else v_even[:, n // 2, :]
                    qs = slice((n % 2) * CHUNK, (n % 2 + 1) * CHUNK)
                    for e in range(2):
                        ins = nc.tensor.matmul(
                            o[e * HD:(e + 1) * HD, :, qs], v[:, g * HD:(g + 1) * HD],
                            probs_t[:, tt, PAIRS * e:PAIRS * (e + 1), qs], start=True, stop=True)
                ins.then_inc(att_done, 1)

            def attention(g, k):
                late = att_late(g)
                for what, tt in {1: [(att_scores, 0)], 2: [(att_scores, 1)],
                                 4 + late: [(att_turn, 0), (att_turn, 1)],
                                 5 + late: [(att_value, 0), (att_value, 1)]}.get(k, []):
                    what(g, tt)

            pe.wait_ge(ident_loaded, 16)
            pe.wait_ge(norm0_loaded, 16)
            nc.tensor.transpose(bank[:, 3, 0:KT], vec_rows[0:KT, 0, :], ident[0:KT, 0:KT]).then_inc(vecs_turned, 1)
            for j in range(2):
                pe.wait_ge(x_loaded[j], 16)
                if j == 1:
                    pe.wait_ge(vecs_ready, 1)
                turn_block(x[:, :, j * NB:(j + 1) * NB], 2 * j)

            def body(slot):
                b = slot.b
                if b == NBLK:
                    return
                if b >= 2:
                    if BLOCKS[b - 2][0] in BY_ACT:
                        pe.wait_ge(evac_act, slot.count(N_EVAC_ACT, -1))
                    else:
                        pe.wait_ge(evac_dve, slot.count(N_EVAC_DVE, -1))
                if b in STATIONARY_STARTS:
                    pe.wait_ge(turned_out, slot.count(N_TURNED, -1, INIT_HALVES))
                for k in range(HALVES):
                    if b == 0:
                        pe.wait_ge(turned_out, k + 1)
                    if b == MIX_OUT0 and k in (2, 5):
                        pe.wait_ge(lru_lo, LRU_BLOCKS - 1 + k // 5)
                    if b == ATT_OUT0 and k == 0:
                        pe.wait_ge(att_lo, TT * (KV - 1))
                    if b == ATT_OUT0 and k == HALVES - 2:
                        pe.wait_ge(att_lo, TT * KV)
                    if b in STATIONARY_STARTS and k == HALVES - 2:
                        pe.wait_ge(turned_out, slot.count(N_TURNED, 0, INIT_HALVES))
                    products(slot, k)
                    if b == 0 and k == 5:
                        pe.wait_ge(vecs_loaded, 144)
                        pe.wait_ge(turned_out, INIT_HALVES)
                        nc.tensor.transpose(bank[:, 2, 0:4 * KT], vec_rows[0:4 * KT, 0, :], ident[0:4 * KT, 0:4 * KT])
                        nc.tensor.transpose(bank[:, 2, 4 * KT:136], vec_rows[0:72, 1, :],
                                            ident[0:72, 0:72]).then_inc(vecs_turned, 1)
                    if b == 0 and k in (1, 3):
                        j = 2 + k // 2
                        pe.wait_ge(x_loaded[j], 16)
                        pe.wait_ge(turned_out, 2 * (j - 1))
                        turn_block(x[:, :, j * NB:(j + 1) * NB], 2 * (j % 2))
                    if b > 0:
                        kind, j = BLOCKS[b - 1]
                        if k == TURN_AT.get(kind):
                            post(slot)
                        if slot.i is None:
                            if kind == "v":
                                retention(j, k)
                            if b in LRU_IN_SLOT and k == 4:
                                lru_gates(LRU_IN_SLOT[b])
                            if kind == "aq":
                                attention(j, k)

            run_slots(pe, body)


_INS = ["x", "norm_mix_w", "norm_mlp_w", "final_norm_w", "hyb_w_in", "ret_norm_w", "lru_conv_w", "lru_conv_b",
        "lru_w_a", "lru_b_a", "lru_w_x", "lru_b_x", "lru_lambda", "hyb_w_out", "attn_w_qkv", "attn_sinks",
        "attn_w_out", "mlp_w_up", "mlp_w_down"]


def kernel(**inputs):
    import concourse.bacc as _bacc
    from concourse.bass_utils import run_bass_kernel_spmd as _run

    nc = _bacc.Bacc("TRN2", target_bir_lowering=False, num_devices=1)
    given = {name: np.ascontiguousarray(inputs[name]) for name in _INS}
    given |= {"ident": np.eye(P, dtype=np.float32), "rope": rope_table(), "decay": decay_table()}
    tensors, arrays = {}, {}
    for name, a in given.items():
        arrays[f"in_{name}"] = a
        tensors[name] = nc.dram_tensor(f"in_{name}", a.shape, mybir.dt.from_np(a.dtype), kind="ExternalInput").ap()
    tensors["out"] = nc.dram_tensor("out_y", (1, SEQ, D_MODEL), F32, kind="ExternalOutput").ap()
    build(nc, tensors)
    r = _run(nc, [arrays], core_ids=[0])
    return r.results[0]["out_y"]
```
